# Optimizing a Trainium2 kernel written in Bass

```python
import jax, jax.numpy as jnp
from jax import lax
import numpy as np

D_MODEL = 1024
BATCH = 1
SEQ = 1024
DEPTH = 1

MEM_LEN = 256
MLA_HEADS = 8
MLA_NOPE = 64
MLA_ROPE = 32
MLA_V = 64
MLA_Q_RANK = 256
MLA_KV_RANK = 128
FOX_HEADS = 8
FOX_HEAD_DIM = 64
MIX_WIDTH = MLA_HEADS * MLA_V + FOX_HEADS * FOX_HEAD_DIM
IN_COLS = MLA_Q_RANK + MLA_KV_RANK + MLA_ROPE + 3 * FOX_HEADS * FOX_HEAD_DIM + FOX_HEADS
X_HEADS = 4
X_HEAD_DIM = D_MODEL // X_HEADS
N_EXPERTS = 32
TOP_K = 4
D_EXPERT = D_MODEL
SWIGLU_LIMIT = 7.0
SWIGLU_ALPHA = 1.702
ROPE_THETA = 10000.0
Q_BLOCK = 128
EPS = 1e-6

kernel_name = "hymba_mla_fox_memxattn_moe"

def rmsnorm(x, g):
    xf = x.astype(jnp.float32)
    y = xf * lax.rsqrt(jnp.mean(xf * xf, axis=-1, keepdims=True) + EPS)
    return (y * g.astype(jnp.float32)).astype(x.dtype)

def rope(x, pos):
    half = x.shape[-1] // 2
    inv = ROPE_THETA ** (-jnp.arange(half, dtype=jnp.float32) / half)
    ang = pos.astype(jnp.float32)[:, None] * inv[None, :]
    cos = jnp.cos(ang).astype(x.dtype)
    sin = jnp.sin(ang).astype(x.dtype)
    x1, x2 = x[..., :half], x[..., half:]
    return jnp.concatenate([x1 * cos - x2 * sin, x2 * cos + x1 * sin], axis=-1)

def causal_block_attention(q, k, v, scale, log_decay=None):
    B, H, S, Dk = q.shape
    nb = S // Q_BLOCK
    q_blocks = q.reshape(B, H, nb, Q_BLOCK, Dk).transpose(2, 0, 1, 3, 4)
    key_pos = jnp.arange(S)
    if log_decay is None:
        xs = (jnp.arange(nb), q_blocks)
    else:
        c_blocks = log_decay.reshape(B, H, nb, Q_BLOCK).transpose(2, 0, 1, 3)
        xs = (jnp.arange(nb), q_blocks, c_blocks)

    def one_block(args):
        i, qi = args[0], args[1]
        s = jnp.einsum('bhqd,bhkd->bhqk', qi, k, preferred_element_type=jnp.float32) * scale
        if log_decay is not None:
            s = s + args[2][..., :, None] - log_decay.astype(jnp.float32)[:, :, None, :]
        q_pos = i * Q_BLOCK + jnp.arange(Q_BLOCK)
        mask = key_pos[None, :] <= q_pos[:, None]
        s = jnp.where(mask, s, jnp.finfo(jnp.float32).min)
        p = jax.nn.softmax(s, axis=-1)
        return jnp.einsum('bhqk,bhkd->bhqd', p.astype(v.dtype), v)

    out = lax.map(one_block, xs)
    return out.transpose(1, 2, 0, 3, 4).reshape(B, H, S, v.shape[-1])

def hybrid_mixer(hn, w_in, q_norm, w_q_up, kv_norm, w_kv_up, b_forget, g_out_mla, g_out_fox, w_o):
    B, S, _ = hn.shape
    proj = hn @ w_in
    fw = FOX_HEADS * FOX_HEAD_DIM
    cuts = list(np.cumsum([MLA_Q_RANK, MLA_KV_RANK, MLA_ROPE, fw, fw, fw]))
    q_lat, kv_lat, k_pe, fq, fk, fv, f_logit = jnp.split(proj, cuts, axis=-1)
    pos = jnp.arange(S)

    q = (rmsnorm(q_lat, q_norm) @ w_q_up).reshape(B, S, MLA_HEADS, MLA_NOPE + MLA_ROPE).transpose(0, 2, 1, 3)
    q_mla = jnp.concatenate([q[..., :MLA_NOPE], rope(q[..., MLA_NOPE:], pos)], axis=-1)
    kv = (rmsnorm(kv_lat, kv_norm) @ w_kv_up).reshape(B, S, MLA_HEADS, MLA_NOPE + MLA_V).transpose(0, 2, 1, 3)
    k_rope = rope(k_pe[:, None, :, :], pos)
    k_mla = jnp.concatenate([kv[..., :MLA_NOPE], jnp.broadcast_to(k_rope, (B, MLA_HEADS, S, MLA_ROPE))], axis=-1)
    v_mla = kv[..., MLA_NOPE:]
    o_mla = causal_block_attention(q_mla, k_mla, v_mla, (MLA_NOPE + MLA_ROPE) ** -0.5)

    heads = lambda t: t.reshape(B, S, FOX_HEADS, FOX_HEAD_DIM).transpose(0, 2, 1, 3)
    log_f = jax.nn.log_sigmoid(f_logit.astype(jnp.float32) + b_forget.astype(jnp.float32))
    c = jnp.cumsum(log_f, axis=1).transpose(0, 2, 1)
    o_fox = causal_block_attention(heads(fq), heads(fk), heads(fv), FOX_HEAD_DIM ** -0.5, c)

    o_mla = o_mla.transpose(0, 2, 1, 3).reshape(B, S, MLA_HEADS * MLA_V)
    o_fox = o_fox.transpose(0, 2, 1, 3).reshape(B, S, fw)
    o = jnp.concatenate([rmsnorm(o_mla, g_out_mla), rmsnorm(o_fox, g_out_fox)], axis=-1)
    return o @ w_o

def memory_cross_attention(hn, mem, mem_norm, w_xq, w_mem_kv, w_xo):
    B, S, _ = hn.shape
    M = mem.shape[1]
    mn = rmsnorm(mem, mem_norm)
    q = (hn @ w_xq).reshape(B, S, X_HEADS, X_HEAD_DIM)
    kv = (mn @ w_mem_kv).reshape(B, M, 2, X_HEADS, X_HEAD_DIM)
    k, v = kv[:, :, 0], kv[:, :, 1]
    s = jnp.einsum('bshd,bmhd->bhsm', q, k, preferred_element_type=jnp.float32) * X_HEAD_DIM ** -0.5
    p = jax.nn.softmax(s, axis=-1)
    o = jnp.einsum('bhsm,bmhd->bshd', p.astype(v.dtype), v).reshape(B, S, D_MODEL)
    return o @ w_xo

def moe_ffn(hn, w_router, b_router, w_gate_up, b_gate_up, w_down, b_down):
    B, S, D = hn.shape
    T = B * S
    xt = hn.reshape(T, D)
    logits = (xt @ w_router).astype(jnp.float32) + b_router.astype(jnp.float32)
    top_vals, top_idx = lax.top_k(logits, TOP_K)
    gates = jax.nn.softmax(top_vals, axis=-1)
    flat_e = top_idx.reshape(-1)
    order = jnp.argsort(flat_e)
    e_sorted = flat_e[order]
    tok = order // TOP_K
    group_sizes = jnp.bincount(flat_e, length=N_EXPERTS).astype(jnp.int32)
    xs = xt[tok]
    h = lax.ragged_dot(xs, w_gate_up, group_sizes) + b_gate_up[e_sorted]
    glu = jnp.minimum(h[:, ::2], SWIGLU_LIMIT)
    lin = jnp.clip(h[:, 1::2], -SWIGLU_LIMIT, SWIGLU_LIMIT)
    act = glu * jax.nn.sigmoid(SWIGLU_ALPHA * glu) * (lin + 1.0)
    y = lax.ragged_dot(act, w_down, group_sizes) + b_down[e_sorted]
    y = y * gates.reshape(-1)[order].astype(y.dtype)[:, None]
    out = jax.ops.segment_sum(y, tok, num_segments=T)
    return out.reshape(B, S, D)

def setup_inputs(seed: int = 0) -> dict:
    key = jax.random.key(seed)
    ks = jax.random.split(key, 32)
    f32 = jnp.float32
    L = DEPTH
    nrm = lambda k, shape, fan_in: jax.random.normal(k, shape, f32) * (fan_in ** -0.5)
    gain = lambda k, shape: 1.0 + 0.02 * jax.random.normal(k, shape, f32)
    small = lambda k, shape: 0.01 * jax.random.normal(k, shape, f32)
    return {
        "x": jax.random.normal(ks[0], (BATCH, SEQ, D_MODEL), f32),
        "mem": jax.random.normal(ks[1], (BATCH, MEM_LEN, D_MODEL), f32),
        "ln_mix": gain(ks[2], (L, D_MODEL)),
        "w_in": nrm(ks[3], (L, D_MODEL, IN_COLS), D_MODEL),
        "q_norm": gain(ks[4], (L, MLA_Q_RANK)),
        "w_q_up": nrm(ks[5], (L, MLA_Q_RANK, MLA_HEADS * (MLA_NOPE + MLA_ROPE)), MLA_Q_RANK),
        "kv_norm": gain(ks[6], (L, MLA_KV_RANK)),
        "w_kv_up": nrm(ks[7], (L, MLA_KV_RANK, MLA_HEADS * (MLA_NOPE + MLA_V)), MLA_KV_RANK),
        "b_forget": jax.random.uniform(ks[8], (L, FOX_HEADS), f32, minval=1.0, maxval=4.0),
        "g_out_mla": gain(ks[9], (L, MLA_HEADS * MLA_V)),
        "g_out_fox": gain(ks[10], (L, FOX_HEADS * FOX_HEAD_DIM)),
        "w_o": nrm(ks[11], (L, MIX_WIDTH, D_MODEL), MIX_WIDTH),
        "ln_cross": gain(ks[12], (L, D_MODEL)),
        "mem_norm": gain(ks[13], (L, D_MODEL)),
        "w_xq": nrm(ks[14], (L, D_MODEL, D_MODEL), D_MODEL),
        "w_mem_kv": nrm(ks[15], (L, D_MODEL, 2 * D_MODEL), D_MODEL),
        "w_xo": nrm(ks[16], (L, D_MODEL, D_MODEL), D_MODEL),
        "ln_ffn": gain(ks[17], (L, D_MODEL)),
        "w_router": nrm(ks[18], (L, D_MODEL, N_EXPERTS), D_MODEL),
        "b_router": small(ks[19], (L, N_EXPERTS)),
        "w_gate_up": nrm(ks[20], (L, N_EXPERTS, D_MODEL, 2 * D_EXPERT), D_MODEL),
        "b_gate_up": small(ks[21], (L, N_EXPERTS, 2 * D_EXPERT)),
        "w_down": nrm(ks[22], (L, N_EXPERTS, D_EXPERT, D_MODEL), D_EXPERT),
        "b_down": small(ks[23], (L, N_EXPERTS, D_MODEL)),
        "ln_final": gain(ks[24], (D_MODEL,)),
    }

def reference(x, mem, ln_mix, w_in, q_norm, w_q_up, kv_norm, w_kv_up, b_forget, g_out_mla, g_out_fox, w_o,
              ln_cross, mem_norm, w_xq, w_mem_kv, w_xo, ln_ffn, w_router, b_router, w_gate_up, b_gate_up,
              w_down, b_down, ln_final):
    h = x
    for l in range(DEPTH):
        h = h + hybrid_mixer(rmsnorm(h, ln_mix[l]), w_in[l], q_norm[l], w_q_up[l], kv_norm[l], w_kv_up[l],
                             b_forget[l], g_out_mla[l], g_out_fox[l], w_o[l])
        h = h + memory_cross_attention(rmsnorm(h, ln_cross[l]), mem, mem_norm[l], w_xq[l], w_mem_kv[l], w_xo[l])
        h = h + moe_ffn(rmsnorm(h, ln_ffn[l]), w_router[l], b_router[l], w_gate_up[l], b_gate_up[l],
                        w_down[l], b_down[l])
    return rmsnorm(h, ln_final)


_drawn_inputs = setup_inputs


def setup_inputs(seed=0):
    import zlib

    import numpy as np

    out = dict(_drawn_inputs(seed))
    spreads = {}
    factors = {'ln_cross': 5.987,
     'mem_norm': 4.406,
     'b_gate_up': 39.974,
     'b_down': 45.84,
     'ln_final': 8.115,
     'ln_ffn': 5.517,
     'b_router': 6.986}
    for name, (base, spread) in spreads.items():
        noise = np.random.default_rng([zlib.crc32(name.encode()), seed]).standard_normal(out[name].shape)
        drawn = base * np.exp(spread * noise) if base else spread * noise
        out[name] = __import__('jax').numpy.asarray(drawn.astype(out[name].dtype))
    for name, factor in factors.items():
        out[name] = (out[name] * factor).astype(out[name].dtype)
    return out
```

```python
from contextlib import ExitStack

import concourse.bass as bass
import numpy as np
from concourse import mybir

F32 = mybir.dt.float32
BF16 = mybir.dt.bfloat16
I32 = mybir.dt.int32
U32 = mybir.dt.uint32
ALU = mybir.AluOpType
ACT = mybir.ActivationFunctionType
AX = mybir.AxisListType.X

P = 128
EPS = 1e-6
MASKED = -1e30


class Handoff:

    def __init__(self, sem, name):
        self.full = sem(name + "_full")
        self.free = sem(name + "_free")
        self.base = 0

    def after(self, fills):
        later = object.__new__(Handoff)
        later.full, later.free, later.base = self.full, self.free, self.base + fills
        return later


def shapes(x, mem, w_q_up, w_router, w_in):
    class S:
        pass

    S.T, S.D = x.shape[1:]
    S.NT, S.KD = S.T // P, S.D // P
    S.M = mem.shape[1]
    S.MT = S.M // P
    S.QR, S.KR, S.RO = 256, 128, 32
    S.H, S.DN, S.DV = 8, 64, 64
    S.DQ = S.DN + S.RO
    S.FW = S.H * S.DV
    S.LAT = S.QR + S.KR + S.RO + S.H
    S.IN = S.LAT + 3 * S.FW
    S.XH, S.XD = 4, S.D // 4
    S.E = w_router.shape[-1]
    S.TOP = 4
    S.CAP = 256
    S.MORE = S.T * S.TOP // (S.CAP + 1)
    S.ITEMS = S.E + S.MORE
    return S


def build(nc, S, a, out):
    T, D, NT, KD, H, FW, E, CAP = S.T, S.D, S.NT, S.KD, S.H, S.FW, S.E, S.CAP
    ctx = ExitStack()
    with ctx:
        def sem(name):
            return ctx.enter_context(nc.semaphore(name))

        base = (nc.sbuf_base + 63) // 64 * 64

        class Region:

            def __init__(self, start, end):
                self.at, self.end = base + int(start * 1024), base + int(end * 1024)

            def __call__(self, name, shape, dt=F32):
                t = nc.alloc_sbuf_tensor_at(name, shape, dt, offset=self.at)
                size = int(np.prod(shape[1:])) * (2 if dt == BF16 else 4)
                self.at += (size + 63) // 64 * 64
                assert self.at <= self.end, (name, (self.at - base) / 1024)
                return t

        keep = Region(0, 15)
        const = keep("const", [P, S.NCONST])
        ident, tri, mask = const[:, 0:P], const[:, P:2 * P], const[:, 2 * P:3 * P]
        iota = const[:, 3 * P:3 * P + CAP]
        pcol = const[:, 3 * P + CAP:3 * P + CAP + 1]
        ident_b = keep("ident_b", [P, P], BF16)
        mask_b = keep("mask_b", [P, P], BF16)
        before_b = keep("before_b", [P, P], BF16)
        ones_b = keep("ones_b", [P, P], BF16)
        ones = keep("ones", [P, P])
        gains = keep("gains", [P, 4 * KD + 3 + KD])
        g_mix, g_cross, g_mem, g_ffn = (gains[:, k * KD:(k + 1) * KD] for k in range(4))
        g_lat, g_out = gains[:, 4 * KD:4 * KD + 3], gains[:, 4 * KD + 3:]
        bf_row = keep("bf_row", [P, H])
        br_row = keep("br_row", [P, E])
        gates = keep("gates", [P, NT, S.TOP])
        key = keep("key", [P, NT, E])
        mv = keep("mv", [P, NT * E * 4], BF16)
        mv4 = mv[:, :].rearrange("p (t e c) -> p t e c", t=NT, e=E)
        shift = keep("shift", [P, S.ITEMS + 2])
        items = keep("items", [P, 3, S.ITEMS + 2], I32)
        half = keep("half", [P, 8])
        h_res = Region(15, 47)("h_res", [P, NT, D])
        km = Region(47, 55)("km", [P, KD, S.M])
        vm = Region(55, 63)("vm", [P, S.MT, D])
        w_mem_k = Region(15, 47)("w_mem_k", [P, KD, D])
        w_mem_v = Region(95, 127)("w_mem_v", [P, KD, D])
        r = Region(63, 95)
        mem_sb = r("mem_sb", [P, S.MT, D])
        mem_n = r("mem_n", [P, S.MT, D])
        mem_t = r("mem_t", [P, KD, S.M])
        mem_ss = r("mem_ss", [P, 4])
        r = Region(63, 95)
        v_mla = r("v_mla", [P, NT, FW])
        v_fox = r("v_fox", [P, NT, FW])
        r = Region(134, 207)
        w_in = r("w_in", [P, KD, S.IN])
        w_qu = r("w_qu", [P, 2, H * S.DQ])
        w_ku = r("w_ku", [P, H * 2 * S.DN])
        r = Region(15, 47)
        x_sb = r("x_sb", [P, D])
        xn = r("xn", [P, D])
        xt = r("xt", [P, KD, P])
        sq_a = r("sq_a", [P, D])
        lat = r("lat", [P, S.LAT])
        latn = r("latn", [P, 3, P])
        lat_t = r("lat_t", [P, 3, P])
        cos = r("cos", [P, NT, S.RO])
        sin = r("sin", [P, NT, S.RO])
        st_a = r("st_a", [P, 16])
        fz = r("fz", [P, 6, H])
        rsum = r("rsum", [P, H])
        assert S.RO == 32
        r = Region(95, 134)
        fq_sb = r("fq_sb", [P, FW])
        fk_sb = r("fk_sb", [P, FW])
        q_sb = r("q_sb", [P, H, S.DQ])
        k_sb = r("k_sb", [P, H, S.DQ])
        rot = r("rot", [P, 2, H, S.RO])
        krot = r("krot", [P, 2, S.RO])
        st_q = [r(f"st_q{g}", [S.DQ, 4, P]) for g in range(4)]
        st_f = [r(f"st_f{g}", [P, 4, P]) for g in range(2)]
        cneg_sb = r("cneg_sb", [H, P])
        w_o = Region(95, 127)("w_o", [P, KD, D])
        o_sb = Region(127, 159)("o_sb", [P, NT, D])
        r = Region(15, 47)
        prob = [r(f"prob{b}", [P, T]) for b in range(2)]
        prob_t = [r(f"prob_t{b}", [P, NT, P]) for b in range(2)]
        biased = [r(f"biased{b}", [P, T]) for b in range(2)]
        cneg = r("cneg", [P, T])
        mx = r("mx", [P, 16])
        nm = r("nm", [P, 16])
        rs = r("rs", [P, 16])
        rr = r("rr", [P, 16])
        r = Region(159, 175)
        qt = [r("qt_mla", [S.DQ, T]), r("qt_fox", [S.DN, T])]
        kt = [r("kt_mla", [S.DQ, T]), r("kt_fox", [S.DN, T])]
        w_xq = Region(175, 207)("w_xq", [P, KD, D])
        r = Region(159, 175)
        on = r("on", [P, D])
        o_t = r("o_t", [P, KD, P])
        x_again = r("x_again", [P, D])
        st_c = r("st_c", [P, 4])
        w_xo = Region(63, 95)("w_xo", [P, KD, D])
        r = Region(143, 175)
        hn = r("hn", [P, D])
        hn_t = r("hn_t", [P, KD, P])
        qx_t = r("qx_t", [P, KD, P])
        px = r("px", [P, S.XH, S.M])
        px_t = r("px_t", [P, KD, P])
        ox_t = r("ox_t", [P, KD, P])
        sq_c = r("sq_c", [P, D])
        st_x = r("st_x", [P, 32])
        r = Region(143, 175)
        rn = r("rn", [P, D])
        rn_t = r("rn_t", [P, KD, P])
        sq_r = r("sq_r", [P, D])
        w_r = r("w_r", [P, KD, E])
        lg = r("lg", [P, E])
        val8 = r("val8", [P, 8])
        idx8 = r("idx8", [P, 8], U32)
        idxf = r("idxf", [P, 8])
        eq = r("eq", [P, S.TOP, E])
        eqj = r("eqj", [P, S.TOP, E])
        jrow = r("jrow", [P, S.TOP])
        st_r = r("st_r", [P, 16])
        sel = r("sel", [P, NT, E])
        sel_b = r("sel_b", [P, NT, E], BF16)
        run_b = r("run_b", [P, NT + 1, E], BF16)
        cnt = r("cnt", [P, E])
        more = r("more", [P, 4, E])
        NQ = S.MORE + 2
        le = r("le", [P, NQ, E])
        le2 = r("le2", [P, NQ, E])
        ov = r("ov", [P, 8, NQ])
        SLOTS = 6
        slots = [Region(95 + 16 * c, 111 + 16 * c)(f"slot{c}", [P, KD, 512]) for c in range(SLOTS)]
        r = Region(63, 95)
        act_t = r("act_t", [P, KD, CAP])
        y_t = r("y_t", [P, KD, CAP])
        y_sb = r("y_sb", [P, 2, D])
        xg = r("xg", [P, 2, D])
        r = Region(47, 63)
        xe_t = r("xe_t", [P, KD, CAP])
        hot = r("hot", [P, NT, CAP], BF16)
        r = Region(191, 207)
        b_gu = r("b_gu", [P, E * 2 * KD])
        b_dn = r("b_dn", [P, E * KD])
        glu = [r(f"glu{b}", [P, CAP]) for b in range(2)]
        lin = [r(f"lin{b}", [P, CAP]) for b in range(2)]
        sig = [r(f"sig{b}", [P, CAP]) for b in range(2)]
        ix = r("ix", [P, 2, 4])
        ixt = r("ixt", [P, 2])
        ixo = r("ixo", [P, 2])
        ixs = r("ixs", [P, 2])
        ixp = r("ixp", [P, 2])
        gidx = r("gidx", [P, 2], I32)
        sidx = r("sidx", [P, 2], I32)
        r = Region(95, 207)
        ye = [r(f"ye{b}", [P, S.TOP, D]) for b in range(2)]
        acc = [r(f"acc{b}", [P, D]) for b in range(2)]
        sq_f = r("sq_f", [P, D])
        g_fin = r("g_fin", [P, D])
        of = [r(f"of{b}", [P, D]) for b in range(2)]
        st_fin = r("st_fin", [P, 8])

        def scratch(name, shape, dt=F32):
            return nc.dram_tensor(name, shape, dt, kind="Internal").ap()

        d_q = scratch("d_q", [H, S.DQ, T])
        d_k = scratch("d_k", [H, S.DQ, T])
        d_fq = scratch("d_fq", [FW, T])
        d_fk = scratch("d_fk", [FW, T])
        d_cneg = scratch("d_cneg", [H, T])
        d_xn = scratch("d_xn", [T, D])
        d_y = scratch("d_y", [T * S.TOP, D])

        bank = [ctx.enter_context(nc.psum_tensor(f"bank{b}", [P, 512], F32)) for b in range(4)]
        wide = [ctx.enter_context(nc.psum_tensor(f"wide{b}", [P, 1024], F32)) for b in range(2)]
        pt = bank[0:2]
        pp = bank[2:4]


        def bank_u(g):
            return wide[0][:, g * 512:(g + 1) * 512]

        bank_c = wide[1]
        pp2 = [wide[0][:, 0:512], wide[0][:, 512:1024]]
        SCALE = [float(S.DQ) ** -0.5, float(S.DN) ** -0.5]
        A_ST = [(1, 2, S.DQ), (0, 3, S.DQ), (1, 3, S.DQ), (0, 4, S.DQ), (1, 4, P), (0, 5, P)]
        A_PT = [5, 4]

        def b_groups():
            used, plan = [0, 0], []
            for n in range(2 * NT):
                mine = []
                for g in range((n % NT) // 4 + 1):
                    b = (n + g) % 2
                    used[b] += 1
                    mine.append((g, b, used[b]))
                plan.append(mine)
            return plan, used

        B_PLAN, B_PT = b_groups()
        B_GRP1 = sum(len(g) > 1 for g in B_PLAN)

        ld = {n: sem("ld_" + n) for n in (
            "small", "mem", "w_mem_k", "w_mem_v", "w_in", "rope", "w_o", "w_xq", "w_xo",
            "w_r", "bias", "g_fin")}
        stage_end, passed = sem("stage_end"), sem("passed")
        init = sem("init")

        ENGINES = 5

        def barrier(eng, n):
            eng.drain().then_inc(stage_end, 1)
            eng.wait_ge(stage_end, ENGINES * n)

        m_ss, m_rs, m_n = sem("m_ss"), sem("m_rs"), sem("m_n")
        m_pt = [Handoff(sem, f"pt{b}") for b in range(2)]
        m_pp = [Handoff(sem, f"pp{b}") for b in range(2)]
        a_pt = [m_pt[b].after(S.MT * KD // 8) for b in range(2)]
        a_pp = [m_pp[b].after((KD // 2 + S.MT * D // 512) // 2) for b in range(2)]
        b_pt = [a_pt[b].after(A_PT[b] * NT) for b in range(2)]
        b_po = [a_pp[b].after(2 * NT) for b in range(2)]
        c_pt = [b_pt[b].after(B_PT[b] * H) for b in range(2)]
        c_pp = [b_po[b].after(NT * H) for b in range(2)]
        x_pt = [c_pt[b].after(NT) for b in range(2)]
        x_pp = [c_pp[b].after(NT) for b in range(2)]
        r_pt = [x_pt[b].after(2 * NT) for b in range(2)]
        e_pt = [r_pt[b].after(NT) for b in range(2)]

        def turn_in_use(b, i, k):
            return e_pt[b].base + k if isinstance(i, int) and i == 0 else e_pt[b].base + 4 * i - 2 + k

        def turn_out_use(b, i, k):
            return e_pt[b].base + 4 * i + 4 + k

        e_gu = [x_pp[b].after(2 * NT) for b in range(2)]

        a_x = Handoff(sem, "a_x")
        a_ss, a_rstd, a_lss, a_lrstd = sem("a_ss"), sem("a_rstd"), sem("a_lss"), sem("a_lrstd")
        a_xn = Handoff(sem, "a_xn")
        a_xt, a_latn, a_latt = sem("a_xt"), sem("a_latn"), sem("a_latt")
        a_pu = [Handoff(sem, f"a_pu{b}") for b in range(2)]
        a_pc = Handoff(sem, "a_pc")
        a_fz, a_fl, a_logf = sem("a_fz"), sem("a_fl"), sem("a_logf")
        a_up, a_qk = sem("a_up"), sem("a_qk")
        a_st = [Handoff(sem, f"a_st{g}") for g in range(7)]

        b_in = [Handoff(sem, f"b_in{y}") for y in range(2)]
        b_cneg = Handoff(sem, "b_cneg")
        b_s = [Handoff(sem, f"b_s{b}") for b in range(2)]
        b_nm = sem("b_nm")
        b_p = [Handoff(sem, f"b_p{b}") for b in range(2)]
        b_ptd, b_pta = sem("b_ptd"), sem("b_pta")

        c_ss, c_rstd = sem("c_ss"), sem("c_rstd")
        c_on = Handoff(sem, "c_on")
        c_x = Handoff(sem, "c_x")
        c_ot = sem("c_ot")

        x_ss, x_rstd, x_hn, x_hnt, x_qx = sem("x_ss"), sem("x_rstd"), sem("x_hn"), sem("x_hnt"), sem("x_qx")
        x_s = Handoff(sem, "x_s")
        x_nm, x_p, x_pn, x_pxt, x_ox = sem("x_nm"), sem("x_p"), sem("x_pn"), sem("x_pxt"), sem("x_ox")
        x_w = [Handoff(sem, f"x_w{b}") for b in range(2)]

        r_ss, r_rstd, r_rnt, r_idx, r_ex, r_sel = (
            sem("r_ss"), sem("r_rstd"), sem("r_rnt"), sem("r_idx"), sem("r_ex"), sem("r_sel"))
        r_rn = Handoff(sem, "r_rn")
        r_st = sem("r_st")
        r_pl = Handoff(sem, "r_pl")
        r_rank = sem("r_rank")
        r_cnt = sem("r_cnt")

        e_w = [Handoff(sem, f"e_w{c}") for c in range(SLOTS)]
        e_hot, e_ix = sem("e_hot"), sem("e_ix")
        e_idx = sem("e_idx")
        e_xg = sem("e_xg")
        e_y = Handoff(sem, "e_y")
        e_left = sem("e_left")
        e_dn = [Handoff(sem, f"e_dn{b}") for b in range(2)]
        e_xt, e_glu, e_sig, e_act, e_yt = sem("e_xt"), sem("e_glu"), sem("e_sig"), sem("e_act"), sem("e_yt")

        f_y = [Handoff(sem, f"f_y{b}") for b in range(2)]
        f_acc, f_ss, f_rstd, f_o = sem("f_acc"), sem("f_ss"), sem("f_rstd"), sem("f_o")
        f_out = [sem(f"f_out{b}") for b in range(2)]

        def apart(eng):
            eng.sem_inc(passed, 1)

        block = ctx.enter_context(nc.Block())

        def rows(w):
            return w.rearrange("(k p) n -> p k n", p=P)

        @block.sync
        def _(sp):
            def load(dst, src, s):
                sp.dma_start(dst, src).then_inc(s, 16)

            load(const[:, :], a["const"], ld["small"])
            load(mem_sb[:, :, :], a["mem"][0].rearrange("(t p) d -> p t d", p=P), ld["mem"])
            load(gains[:, :], a["gains"], ld["small"])
            load(bf_row[:, :], a["b_forget"][0].partition_broadcast(P), ld["small"])
            load(br_row[:, :], a["b_router"][0].partition_broadcast(P), ld["small"])
            load(w_mem_k[:, :, :], rows(a["w_mem_kv"][0])[:, :, 0:D], ld["w_mem_k"])
            load(w_mem_v[:, :, :], rows(a["w_mem_kv"][0])[:, :, D:2 * D], ld["w_mem_v"])
            w = rows(a["w_in"][0])
            cut = S.LAT - H
            load(w_in[:, :, 0:cut], w[:, :, 0:cut], ld["w_in"])
            load(w_in[:, :, cut:S.LAT], w[:, :, S.IN - H:S.IN], ld["w_in"])
            load(w_in[:, :, S.LAT:S.IN], w[:, :, cut:S.IN - H], ld["w_in"])
            load(w_qu[:, :, :], rows(a["w_q_up"][0]), ld["w_in"])
            load(w_ku[:, :], a["w_kv_up"][0], ld["w_in"])
            barrier(sp, 1)

            load(cos[:, :, :], a["cos"].rearrange("(t p) c -> p t c", p=P), ld["rope"])
            load(sin[:, :, :], a["sin"].rearrange("(t p) c -> p t c", p=P), ld["rope"])
            def load_x(i):
                sp.wait_ge(a_x.free, i + 1)
                load(x_sb[:, :], a["x"][0, bass.ds(i * P, P), :], a_x.full)

            def store_qk(i):
                for g in range(4):
                    dst = (d_q, d_k)[g // 2]
                    h0 = 4 * (g % 2)
                    sp.wait_ge(a_st[g].full, i + 1)
                    sp.dma_start(dst[h0:h0 + 4, :, bass.ds(i * P, P)].rearrange("h d t -> d h t"),
                                 st_q[g][:, :, :]).then_inc(a_st[g].free, 16)
                for g in range(2):
                    dst = (d_fq, d_fk)[g]
                    sp.wait_ge(a_st[4 + g].full, i + 1)
                    sp.dma_start(dst[:, bass.ds(i * P, P)].rearrange("(c p) t -> p c t", p=P),
                                 st_f[g][:, :, :]).then_inc(a_st[4 + g].free, 16)
                sp.wait_ge(a_st[6].full, i + 1)
                sp.dma_start(d_cneg[:, bass.ds(i * P, P)], cneg_sb[:, :]).then_inc(a_st[6].free, 16)

            load_x(0)
            with sp.Fori(0, NT - 1) as i:
                load_x(i + 1)
                store_qk(i)
            store_qk(NT - 1)
            for g in range(7):
                sp.wait_ge(a_st[g].free, 16 * (NT + 1))
            barrier(sp, 2)

            load(w_o[:, :, :], rows(a["w_o"][0]), ld["w_o"])
            with sp.Fori(0, H) as h:
                for y in range(2):
                    sp.wait_ge(b_in[y].free, h + 1)
                    src = ((d_q, d_k), (d_fq, d_fk))[y]
                    for dst, s in zip((qt[y], kt[y]), src):
                        s = s[bass.ds(h, 1), :, :].rearrange("h d t -> (h d) t") if y == 0 \
                            else s[bass.ds(h * S.DN, S.DN), :]
                        load(dst[:, :], s, b_in[y].full)
                sp.wait_ge(b_cneg.free, h + 1)
                load(cneg[:, :], d_cneg[bass.ds(h, 1), :].to_broadcast([P, T]), b_cneg.full)
            load(w_xq[:, :, :], rows(a["w_xq"][0]), ld["w_xq"])
            barrier(sp, 3)

            load(w_xo[:, :, :], rows(a["w_xo"][0]), ld["w_xo"])
            with sp.Fori(0, NT) as i:
                sp.wait_ge(c_x.free, i + 1)
                load(x_again[:, :], a["x"][0, bass.ds(i * P, P), :], c_x.full)
            barrier(sp, 4)

            def expert_part(c, e):
                if c < 4:
                    return a["w_gu"][bass.ds(e * 4 + c, 1), :, :, :].rearrange("a p k n -> (a p) k n")
                return a["w_dn"][bass.ds(e * 2 + c - 4, 1), :, :, :].rearrange("a p k n -> (a p) k n")

            for c in range(3):
                load(slots[c][:, :, :], expert_part(c, 0), e_w[c].full)
            barrier(sp, 5)

            load(w_r[:, :, :], rows(a["w_router"][0]), ld["w_r"])
            with sp.Fori(0, NT) as i:
                sp.wait_ge(r_rn.full, i + 1)
                sp.dma_start(d_xn[bass.ds(i * P, P), :], rn[:, :]).then_inc(r_st, 16)
            sp.wait_ge(r_st, 16 * (NT + 1))
            barrier(sp, 6)

            load(b_gu[:, :], a["b_gu"], ld["bias"])
            load(b_dn[:, :], a["b_dn"], ld["bias"])
            for c in range(3, SLOTS):
                load(slots[c][:, :, :], expert_part(c, 0), e_w[c].full)

            def refill(i, e):
                for c in range(SLOTS):
                    sp.wait_ge(e_w[c].free, i)
                    load(slots[c][:, :, :], expert_part(c, e), e_w[c].full)

            with sp.Fori(1, E) as i:
                refill(i, i)
            with sp.Fori(E, S.ITEMS) as i:
                active = sp.value_load(items[0:1, 2, bass.ds(i, 1)], min_val=0, max_val=1)
                with sp.If(active > 0):
                    e = sp.value_load(items[0:1, 0, bass.ds(i, 1)], min_val=0, max_val=E - 1)
                    refill(i, e)
            barrier(sp, 7)

            load(g_fin[:, :], a["ln_final"].partition_broadcast(P), ld["g_fin"])
            yt = d_y.rearrange("(i p c) d -> i p c d", p=P, c=S.TOP)
            with sp.Fori(0, NT // 2) as u:
                i = 2 * u
                for b in range(2):
                    sp.wait_ge(f_y[b].free, i + 2)
                    load(ye[b][:, :, :], yt[bass.ds(i + b, 1), :, :, :].rearrange("i p c d -> (i p) c d"),
                         f_y[b].full)

        @block.gpsimd
        def _(po):
            po.memset(half[:, :], -0.5).then_inc(init, 1)
            po.memset(ones[:, :], 1.0).then_inc(init, 1)
            po.memset(ones_b[:, :], 1.0).then_inc(init, 1)
            po.memset(mv[:, :], 1.0)
            po.drain()
            for t in range(NT):
                po.memset(mv4[:, t, :, 1], float(P * t))
            po.wait_ge(ld["small"], 64)
            po.tensor_copy(mv[:, :].rearrange("p (n c) -> p n c", c=4)[:, :, 0], pcol.to_broadcast([P, NT * E]))
            po.tensor_copy(ident_b[:, :], ident).then_inc(init, 1)
            po.tensor_copy(mask_b[:, :], mask).then_inc(init, 1)
            po.tensor_tensor(before_b[:, :], tri, ident, ALU.subtract).then_inc(init, 1)

            def power(dst, src, n, k):
                po.tensor_scalar(dst, src, 1.0 / n, EPS, ALU.mult, ALU.add)
                po.drain()
                return po.tensor_tensor(dst, dst, half[:, 0:k], ALU.pow)

            po.wait_ge(m_ss, S.MT)
            power(mem_ss[:, 2:2 + S.MT], mem_ss[:, 0:S.MT], D, S.MT).then_inc(m_rs, 1)
            barrier(po, 1)

            def a_latent(i):
                po.wait_ge(a_lss, i + 1)
                apart(po)
                power(st_a[:, 6:7], st_a[:, 2:3], S.QR, 1)
                power(st_a[:, 7:8], st_a[:, 3:4], S.KR, 1).then_inc(a_lrstd, 1)

            def a_pre(i):
                po.wait_ge(a_ss, i + 1)
                apart(po)
                power(st_a[:, 4:5], st_a[:, 0:1], D, 1).then_inc(a_rstd, 1)

            a_pre(0)
            with po.Fori(0, NT - 1) as i:
                a_latent(i)
                a_pre(i + 1)
            a_latent(NT - 1)
            barrier(po, 2)
            barrier(po, 3)

            with po.Fori(0, NT) as i:
                po.wait_ge(c_ss, i + 1)
                apart(po)
                power(st_c[:, 2:4], st_c[:, 0:2], FW, 2).then_inc(c_rstd, 1)
            barrier(po, 4)
            with po.Fori(0, NT) as i:
                po.wait_ge(x_ss, i + 1)
                apart(po)
                power(st_x[:, 1:2], st_x[:, 0:1], D, 1).then_inc(x_rstd, 1)
            barrier(po, 5)
            with po.Fori(0, NT) as i:
                po.wait_ge(r_ss, i + 1)
                apart(po)
                power(st_r[:, 1:2], st_r[:, 0:1], D, 1).then_inc(r_rstd, 1)
            barrier(po, 6)

            po.memset(xg[:, :, :], 0.0)
            po.drain()

            def gather(i):
                po.wait_ge(e_idx, i + 1)
                apart(po)
                for hb in range(2):
                    po.indirect_dma_start(
                        out=xg[:, hb, :], out_offset=None, in_=d_xn,
                        in_offset=bass.IndirectOffsetOnAxis(ap=gidx[:, hb:hb + 1], axis=0),
                        bounds_check=T - 1, oob_is_err=False).then_inc(e_xg, 16)

            def scatter(i):
                po.wait_ge(e_y.full, i + 1)
                apart(po)
                for hb in range(2):
                    po.indirect_dma_start(
                        out=d_y, out_offset=bass.IndirectOffsetOnAxis(ap=sidx[:, hb:hb + 1], axis=0),
                        in_=y_sb[:, hb, :], in_offset=None,
                        bounds_check=T * S.TOP - 1, oob_is_err=False).then_inc(e_y.free, 16)
                po.wait_ge(e_y.free, 32 * (i + 1))
                po.sem_inc(e_left, 1)

            po.sem_inc(e_left, 1)
            gather(0)
            gather(1)
            with po.Fori(1, E) as i:
                gather(i + 1)
                scatter(i - 1)
            scatter(E - 1)
            with po.Fori(E, S.ITEMS) as i:
                active = po.value_load(items[0:1, 2, bass.ds(i, 1)], min_val=0, max_val=1)
                with po.If(active > 0):
                    gather(i + 1)
                    scatter(i)
            po.sem_inc(f_out[0], 16)
            po.sem_inc(f_out[1], 16)
            barrier(po, 7)
            with po.Fori(0, NT) as i:
                po.wait_ge(f_ss, i + 1)
                apart(po)
                power(st_fin[:, 1:2], st_fin[:, 0:1], D, 1).then_inc(f_rstd, 1)


        @block.scalar
        def _(ac):
            ac.wait_ge(ld["mem"], 16)
            for t in range(S.MT):
                ac.activation(mem_n[:, t, :], mem_sb[:, t, :], ACT.Square, accum_out=mem_ss[:, t:t + 1])
                ac.drain().then_inc(m_ss, 1)
            ac.wait_ge(m_rs, 1)
            for t in range(S.MT):
                ac.activation(mem_n[:, t, :], mem_sb[:, t, :], ACT.Copy, scale=mem_ss[:, 2 + t:3 + t]).then_inc(m_n, 1)
            barrier(ac, 1)

            for g in range(7):
                ac.sem_inc(a_st[g].free, 16)
            for hd in (a_x, a_pc, *a_pu):
                ac.sem_inc(hd.free, 1)
            ac.sem_inc(a_xn.free, 1)

            def a_pre(i):
                ac.wait_ge(a_x.full, 16 * (i + 1))
                ac.activation(sq_a[:, :], x_sb[:, :], ACT.Square, accum_out=st_a[:, 0:1])
                ac.drain().then_inc(a_ss, 1)
                ac.wait_ge(a_rstd, i + 1)
                ac.wait_ge(a_xn.free, i + 1)
                ac.activation(xn[:, :], x_sb[:, :], ACT.Copy, scale=st_a[:, 4:5]).then_inc(a_xn.full, 1)
                ac.drain().then_inc(a_x.free, 1)

            def a_main(i, pre):
                ac.wait_ge(a_fz, i + 1)
                ac.activation(sq_a[:, 0:S.QR], lat[:, 0:S.QR], ACT.Square, accum_out=st_a[:, 2:3])
                ac.activation(sq_a[:, S.QR:S.QR + S.KR], lat[:, S.QR:S.QR + S.KR], ACT.Square,
                              accum_out=st_a[:, 3:4])
                ac.drain().then_inc(a_lss, 1)
                ac.activation(fz[:, 2, :], fz[:, 1, :], ACT.Exp)
                ac.drain()
                ac.activation(fz[:, 3, :], fz[:, 2, :], ACT.Ln, bias=1.0).then_inc(a_fl, 1)
                ac.wait_ge(a_pp[1].full, a_pp[1].base + 2 * i + 1)
                ac.activation(fq_sb[:, :], pp[1][:, :], ACT.Copy).then_inc(a_pp[1].free, 1)
                if pre:
                    a_pre(i + 1)
                ac.wait_ge(a_pp[0].full, a_pp[0].base + 2 * i + 2)
                ac.activation(fk_sb[:, :], pp[0][:, :], ACT.Copy).then_inc(a_pp[0].free, 1)
                hq = H // 2
                for g in range(2):
                    ac.wait_ge(a_pu[g].full, 2 * i + 1)
                    ac.activation(q_sb[:, hq * g:hq * (g + 1), :],
                                  bank_u(g)[:, 0:hq * S.DQ].rearrange("p (h c) -> p h c", h=hq),
                                  ACT.Copy).then_inc(a_pu[g].free, 1)
                for g in range(2):
                    ac.wait_ge(a_pu[g].full, 2 * i + 2)
                    kv = bank_u(g).rearrange("p (h c) -> p h c", h=hq)
                    ac.activation(k_sb[:, hq * g:hq * (g + 1), 0:S.DN], kv[:, :, 0:S.DN], ACT.Copy)
                    ac.activation(
                        v_mla[:, bass.ds(i, 1), hq * g * S.DV:hq * (g + 1) * S.DV].rearrange(
                            "p o (h c) -> p (o h) c", h=hq),
                        kv[:, :, S.DN:], ACT.Copy).then_inc(a_pu[g].free, 1)
                ac.drain().then_inc(a_up, 1)
                ac.wait_ge(a_pp[1].full, a_pp[1].base + 2 * i + 2)
                ac.activation(v_fox[:, bass.ds(i, 1), :].rearrange("p o c -> p (o c)"), pp[1][:, :],
                              ACT.Copy).then_inc(a_pp[1].free, 1)
                for g, (b, k, top) in enumerate(A_ST):
                    ac.wait_ge(a_st[g].free, 16 * (i + 1))
                    ac.wait_ge(a_pt[b].full, a_pt[b].base + A_PT[b] * i + k)
                    dst = (*st_q, *st_f)[g]
                    ac.activation(dst[:, :, :], pt[b][0:top, :].rearrange("p (h t) -> p h t", h=4),
                                  ACT.Copy).then_inc(a_pt[b].free, 1)
                    ac.drain().then_inc(a_st[g].full, 1)

            a_pre(0)
            with ac.Fori(0, NT - 1) as i:
                a_main(i, True)
            a_main(NT - 1, False)
            barrier(ac, 2)

            for hd in (*b_in, b_cneg, *b_s, *b_p):
                ac.sem_inc(hd.free, 1)

            def b_exp(h, n):
                y, i, b = n // NT, n % NT, n % 2
                L = P * (i + 1)
                ac.wait_ge(b_nm, 2 * NT * h + n + 1)
                ac.wait_ge(b_p[b].free, NT * h + n // 2 + 1)
                src = wide[b] if y == 0 else biased[b]
                e = ac.activation(prob[b][:, 0:L], src[:, 0:L], ACT.Exp, bias=nm[:, n:n + 1], scale=SCALE[y],
                                  accum_out=rs[:, n:n + 1])
                if y == 0:
                    e.then_inc(b_s[b].free, 1)
                ac.drain().then_inc(b_p[b].full, 1)

            def b_second(h, n):
                if len(B_PLAN[n]) > 1:
                    g, b, k = B_PLAN[n][1]
                    ac.wait_ge(b_pt[b].full, b_pt[b].base + B_PT[b] * h + k)
                    m = (n % NT) - 3
                    ac.activation(prob_t[n % 2][:, 4:4 + m, :].rearrange("p k t -> p (k t)"), pt[b][:, 0:m * P],
                                  ACT.Copy).then_inc(b_pt[b].free, 1)
                    ac.drain().then_inc(b_pta, 1)

            with ac.Fori(0, H) as h:
                b_exp(h, 0)
                for n in range(2 * NT):
                    if n + 1 < 2 * NT:
                        b_exp(h, n + 1)
                    b_second(h, n)
            barrier(ac, 3)

            for hd in (c_on, c_x):
                ac.sem_inc(hd.free, 1)

            def c_pre(i):
                ot = o_sb[:, bass.ds(i, 1), :].rearrange("p o c -> p (o c)")
                ac.wait_ge(c_on.free, i + 1)
                for g in range(2):
                    ac.activation(on[:, g * FW:(g + 1) * FW], ot[:, g * FW:(g + 1) * FW], ACT.Square,
                                  accum_out=st_c[:, g:g + 1])
                ac.drain().then_inc(c_ss, 1)
                ac.wait_ge(c_rstd, i + 1)
                apart(ac)
                for g in range(2):
                    ac.activation(on[:, g * FW:(g + 1) * FW], ot[:, g * FW:(g + 1) * FW], ACT.Copy,
                                  scale=st_c[:, 2 + g:3 + g])
                ac.drain().then_inc(c_on.full, 1)

            with ac.Fori(0, NT) as i:
                c_pre(i)
            barrier(ac, 4)

            for hd in (x_s, *x_w):
                ac.sem_inc(hd.free, 1)

            def x_pre(i):
                ht = h_res[:, bass.ds(i, 1), :].rearrange("p o c -> p (o c)")
                ac.activation(sq_c[:, :], ht, ACT.Square, accum_out=st_x[:, 0:1])
                ac.drain().then_inc(x_ss, 1)
                ac.wait_ge(x_rstd, i + 1)
                apart(ac)
                ac.activation(hn[:, :], ht, ACT.Copy, scale=st_x[:, 1:2]).then_inc(x_hn, 1)

            def x_main(i, pre):
                for g in range(2):
                    ac.wait_ge(x_pp[g].full, x_pp[g].base + 2 * i + 1)
                    ac.activation(qx_t[:, 4 * g:4 * g + 4, :].rearrange("p k t -> p (k t)"), pp[g][:, :],
                                  ACT.Copy).then_inc(x_pp[g].free, 1)
                ac.drain().then_inc(x_qx, 1)
                ac.wait_ge(x_nm, i + 1)
                for hh in range(S.XH):
                    e = ac.activation(px[:, hh, :], wide[0][:, hh * S.M:(hh + 1) * S.M], ACT.Exp,
                                      bias=st_x[:, 8 + hh:9 + hh], scale=float(S.XD) ** -0.5,
                                      accum_out=st_x[:, 12 + hh:13 + hh])
                e.then_inc(x_s.free, 1)
                ac.drain().then_inc(x_p, 1)
                if pre:
                    x_pre(i + 1)
                for g in range(2):
                    ac.wait_ge(x_pp[g].full, x_pp[g].base + 2 * i + 2)
                    ac.activation(ox_t[:, 4 * g:4 * g + 4, :].rearrange("p k t -> p (k t)"), pp[g][:, :],
                                  ACT.Copy).then_inc(x_pp[g].free, 1)
                ac.drain().then_inc(x_ox, 1)

            x_pre(0)
            with ac.Fori(0, NT - 1) as i:
                x_main(i, True)
            x_main(NT - 1, False)
            barrier(ac, 5)

            for hd in (r_rn, r_pl):
                ac.sem_inc(hd.free, 1)
            ac.sem_inc(r_st, 16)

            def r_pre(i):
                ht = h_res[:, bass.ds(i, 1), :].rearrange("p o c -> p (o c)")
                ac.activation(sq_r[:, :], ht, ACT.Square, accum_out=st_r[:, 0:1])
                ac.drain().then_inc(r_ss, 1)
                ac.wait_ge(r_rstd, i + 1)
                ac.wait_ge(r_rn.free, i + 1)
                ac.wait_ge(r_st, 16 * (i + 1))
                apart(ac)
                ac.activation(rn[:, :], ht, ACT.Copy, scale=st_r[:, 1:2])
                ac.drain().then_inc(r_rn.full, 1)

            def r_gate(i):
                ac.wait_ge(r_idx, i + 1)
                gt = gates[:, bass.ds(i, 1), :].rearrange("p o c -> p (o c)")
                ac.activation(gt, val8[:, 0:S.TOP], ACT.Exp, bias=st_r[:, 4:5], accum_out=st_r[:, 5:6])
                ac.drain().then_inc(r_ex, 1)

            r_pre(0)
            with ac.Fori(0, NT - 1) as i:
                r_pre(i + 1)
                r_gate(i)
            r_gate(NT - 1)
            barrier(ac, 6)

            for hd in e_dn:
                ac.sem_inc(hd.free, 1)
            ac.wait_ge(ld["bias"], 32)

            def rows_back(i):
                ac.wait_ge(e_left, i + 1)
                for g in range(4):
                    b, k = g % 2, g // 2 + 1
                    ac.wait_ge(e_pt[b].full, turn_out_use(b, i, k))
                    hb, half_d = g // 2, g % 2
                    ac.activation(y_sb[:, hb, half_d * 512:(half_d + 1) * 512], pt[b][:, :],
                                  ACT.Copy).then_inc(e_pt[b].free, 1)
                ac.drain().then_inc(e_y.full, 1)

            def step(i, e, before):
                for m in range(KD):
                    ac.wait_ge(e_glu, KD * i + m + 1)
                    ac.activation(sig[m % 2][:, :], glu[m % 2][:, :], ACT.Sigmoid, scale=1.702).then_inc(e_sig, 1)
                    if m == 1 and before is not None:
                        rows_back(before)
                for m in range(KD):
                    b, k = (m // 2) % 2, m // 4 + 1
                    if m % 2 == 0:
                        ac.wait_ge(e_dn[b].full, 2 * i + k)
                    x = ac.activation(y_t[:, m, :], pp2[b][:, (m % 2) * CAP:(m % 2 + 1) * CAP], ACT.Identity,
                                      bias=b_dn[:, bass.ds(e * KD + m, 1)])
                    if m % 2 == 1:
                        x.then_inc(e_dn[b].free, 1)
                    if m % 4 == 3:
                        ac.sem_inc(e_w[4 + m // 4].free, 1)
                ac.drain().then_inc(e_yt, 1)

            step(0, 0, None)
            with ac.Fori(1, E) as i:
                step(i, i, i - 1)
            rows_back(E - 1)
            with ac.Fori(E, S.ITEMS) as i:
                active = ac.value_load(items[0:1, 2, bass.ds(i, 1)], min_val=0, max_val=1)
                with ac.If(active > 0):
                    e = ac.value_load(items[0:1, 0, bass.ds(i, 1)], min_val=0, max_val=E - 1)
                    step(i, e, None)
                    rows_back(i)
            barrier(ac, 7)

            with ac.Fori(0, NT // 2) as u:
                i = 2 * u
                for b in range(2):
                    ac.wait_ge(f_acc, i + b + 1)
                    ac.activation(sq_f[:, :], acc[b][:, :], ACT.Square, accum_out=st_fin[:, 0:1])
                    ac.drain().then_inc(f_ss, 1)
                    ac.wait_ge(f_o, i + b + 1)
                    ac.dma_start(out[0, bass.ds((i + b) * P, P), :], of[b][:, :]).then_inc(f_out[b], 16)
            for b in range(2):
                ac.wait_ge(f_out[b], 16 * (NT // 2) + 16)

        @block.tensor
        def _(pe):
            def transposes(dst, srcs, idn):
                for j, s in enumerate(srcs):
                    m = pe.transpose(dst[0:s.shape[-1], j * P:j * P + s.shape[0]], s, idn)
                return m

            def product(dst, parts, n=None):
                n = n or len(parts)
                for k, (l, r_) in enumerate(parts):
                    m = pe.matmul(dst, l, r_, start=(k == 0), stop=(k == n - 1))
                return m

            pe.wait_ge(init, 6)
            pe.wait_ge(ld["small"], 64)
            pe.wait_ge(m_n, S.MT)
            n = 0
            for t in range(S.MT):
                for g in range(KD // 4):
                    b = n % 2
                    pe.wait_ge(m_pt[b].free, n // 2 + 1)
                    transposes(pt[b], [mem_n[:, t, (4 * g + j) * P:(4 * g + j + 1) * P] for j in range(4)],
                               ident).then_inc(m_pt[b].full, 1)
                    n += 1
            pe.wait_ge(m_rs, 1 + n)
            pe.wait_ge(ld["w_mem_k"], 16)
            n = 0
            for g in range(KD // 2):
                b = n % 2
                pe.wait_ge(m_pp[b].free, n // 2 + 1)
                for j in range(2):
                    c = 2 * g + j
                    m = product(pp[b][:, j * S.M:(j + 1) * S.M],
                                [(w_mem_k[:, k, c * P:(c + 1) * P], mem_t[:, k, :]) for k in range(KD)])
                m.then_inc(m_pp[b].full, 1)
                n += 1
            pe.wait_ge(ld["w_mem_v"], 16)
            for t in range(S.MT):
                for g in range(D // 512):
                    b = n % 2
                    pe.wait_ge(m_pp[b].free, n // 2 + 1)
                    product(pp[b][:, :], [(mem_t[:, k, t * P:(t + 1) * P], w_mem_v[:, k, g * 512:(g + 1) * 512])
                                          for k in range(KD)]).then_inc(m_pp[b].full, 1)
                    n += 1
            barrier(pe, 1)

            pe.wait_ge(ld["w_in"], 80)

            def turn(i, b, k, srcs, idn):
                pe.wait_ge(a_pt[b].free, a_pt[b].base + A_PT[b] * i + k)
                return transposes(pt[b], srcs, idn).then_inc(a_pt[b].full, 1)

            def project(i, b, k, c0, c1):
                pe.wait_ge(a_pp[b].free, a_pp[b].base + 2 * i + k)
                product(pp[b][:, 0:c1 - c0], [(xt[:, kk, :], w_in[:, kk, c0:c1]) for kk in range(KD)])\
                    .then_inc(a_pp[b].full, 1)

            with pe.Fori(0, NT) as i:
                pe.wait_ge(a_xn.full, i + 1)
                turn(i, 0, 1, [xn[:, j * P:(j + 1) * P] for j in range(4)], ident)
                turn(i, 1, 1, [xn[:, j * P:(j + 1) * P] for j in range(4, 8)], ident)
                pe.wait_ge(a_xt, i + 1)
                project(i, 0, 1, 0, S.LAT)
                project(i, 1, 1, S.LAT, S.LAT + FW)
                pe.wait_ge(a_latn, i + 1)
                turn(i, 0, 2, [latn[:, j, :] for j in range(3)], ident)
                project(i, 0, 2, S.LAT + FW, S.LAT + 2 * FW)
                pe.wait_ge(a_latt, i + 1)
                hq = H // 2
                for g in range(2):
                    pe.wait_ge(a_pu[g].free, 2 * i + 1)
                    w = hq * S.DQ
                    product(bank_u(g)[:, 0:w], [(lat_t[:, kk, :], w_qu[:, kk, g * w:(g + 1) * w]) for kk in range(2)])\
                        .then_inc(a_pu[g].full, 1)
                for g in range(2):
                    pe.wait_ge(a_pu[g].free, 2 * i + 2)
                    product(bank_u(g), [(lat_t[:, 2, :], w_ku[:, g * 512:(g + 1) * 512])]).then_inc(a_pu[g].full, 1)
                project(i, 1, 2, S.LAT + 2 * FW, S.IN)
                pe.wait_ge(a_logf, i + 1)
                pe.wait_ge(a_pc.free, i + 1)
                product(bank_c[0:H, 0:P], [(fz[:, 5, :], tri), (rsum[:, :], ones[:, :])]).then_inc(a_pc.full, 1)
                pe.wait_ge(a_qk, i + 1)
                for g, (b, k, _) in enumerate(A_ST[0:4]):
                    src = (q_sb, k_sb)[g // 2]
                    turn(i, b, k, [src[:, 4 * (g % 2) + j, :] for j in range(4)], ident)
                for g, (b, k, _) in enumerate(A_ST[4:6]):
                    src = (fq_sb, fk_sb)[g]
                    turn(i, b, k, [src[:, j * P:(j + 1) * P] for j in range(4)], ident)
            barrier(pe, 2)

            def scores(h, n, after=None):
                y, i, b = n // NT, n % NT, n % 2
                L = P * (i + 1)
                if i == 0:
                    pe.wait_ge(b_in[y].full, 32 * (h + 1))
                pe.wait_ge(b_s[b].free, NT * h + n // 2 + 1)
                ql = qt[y][:, i * P:(i + 1) * P]
                for c in range(0, L, 512):
                    w = min(512, L - c)
                    last = c + w == L
                    m = pe.matmul(wide[b][:, c:c + w], ql, kt[y][:, c:c + w], start=True, stop=not last)
                    if c == 0 and after is not None:
                        m.then_inc(after, 1)
                    elif last and i == NT - 1:
                        m.then_inc(b_in[y].free, 1)
                m = pe.matmul(wide[b][:, L - P:L], ident_b[:, :], mask_b[:, :], start=False, stop=True)
                m.then_inc(b_s[b].full, 1)

            with pe.Fori(0, H) as h:
                scores(h, 0)
                scores(h, 1)
                grp1 = 0
                for n in range(2 * NT):
                    y, i, b = n // NT, n % NT, n % 2
                    pe.wait_ge(b_p[b].full, NT * h + n // 2 + 1)
                    for g, tb, k in B_PLAN[n]:
                        pe.wait_ge(b_pt[tb].free, b_pt[tb].base + B_PT[tb] * h + k)
                        m = transposes(pt[tb], [prob[b][:, j * P:(j + 1) * P] for j in range(4 * g, min(4 * g + 4, i + 1))],
                                       ident)
                        m.then_inc(b_pt[tb].full, 1)
                    if n + 2 < 2 * NT:
                        scores(h, n + 2, b_p[b].free)
                    pe.wait_ge(b_ptd, 2 * NT * h + n + 1)
                    if len(B_PLAN[n]) > 1:
                        grp1 += 1
                        pe.wait_ge(b_pta, B_GRP1 * h + grp1)
                    pe.wait_ge(b_po[b].free, b_po[b].base + NT * h + n // 2 + 1)
                    v = (v_mla, v_fox)[y]
                    for j in range(i + 1):
                        m = pe.matmul(pp[b][:, 0:S.DV], prob_t[b][:, j, :], v[:, j, bass.ds(h * S.DV, S.DV)],
                                      start=j == 0, stop=j == i)
                        if j == 0 and n + 2 >= 2 * NT:
                            m.then_inc(b_p[b].free, 1)
                    m.then_inc(b_po[b].full, 1)
            barrier(pe, 3)

            pe.wait_ge(ld["w_o"], 16)
            with pe.Fori(0, NT) as i:
                pe.wait_ge(c_on.full, i + 1)
                for g in range(2):
                    pe.wait_ge(c_pt[g].free, c_pt[g].base + i + 1)
                    transposes(pt[g], [on[:, j * P:(j + 1) * P] for j in range(4 * g, 4 * g + 4)], ident)\
                        .then_inc(c_pt[g].full, 1)
                pe.wait_ge(c_ot, i + 1)
                for g in range(2):
                    pe.wait_ge(c_pp[g].free, c_pp[g].base + i + 1)
                    product(pp[g][:, :], [(o_t[:, k, :], w_o[:, k, g * 512:(g + 1) * 512]) for k in range(KD)])\
                        .then_inc(c_pp[g].full, 1)
            barrier(pe, 4)

            pe.wait_ge(ld["w_xq"], 16)
            pe.wait_ge(ld["w_xo"], 16)

            def x_out(i):
                pe.wait_ge(x_ox, i + 1)
                for g in range(2):
                    pe.wait_ge(x_w[g].free, i + 1)
                    product(wide[1][:, g * 512:(g + 1) * 512],
                            [(ox_t[:, k, :], w_xo[:, k, g * 512:(g + 1) * 512]) for k in range(KD)])\
                        .then_inc(x_w[g].full, 1)

            def x_body(i, before):
                pe.wait_ge(x_hn, i + 1)
                for g in range(2):
                    pe.wait_ge(x_pt[g].free, x_pt[g].base + 2 * i + 1)
                    transposes(pt[g], [hn[:, j * P:(j + 1) * P] for j in range(4 * g, 4 * g + 4)], ident)\
                        .then_inc(x_pt[g].full, 1)
                pe.wait_ge(x_hnt, i + 1)
                for g in range(2):
                    pe.wait_ge(x_pp[g].free, x_pp[g].base + 2 * i + 1)
                    for j in range(4):
                        c = 4 * g + j
                        m = product(pp[g][:, j * P:(j + 1) * P],
                                    [(w_xq[:, k, c * P:(c + 1) * P], hn_t[:, k, :]) for k in range(KD)])
                    m.then_inc(x_pp[g].full, 1)
                pe.wait_ge(x_qx, i + 1)
                pe.wait_ge(x_s.free, i + 1)
                dc = S.XD // P
                for hh in range(S.XH):
                    m = product(wide[0][:, hh * S.M:(hh + 1) * S.M],
                                [(qx_t[:, hh * dc + c, :], km[:, hh * dc + c, :]) for c in range(dc)])
                m.then_inc(x_s.full, 1)
                if before is not None:
                    x_out(before)
                pe.wait_ge(x_pn, i + 1)
                for g in range(2):
                    pe.wait_ge(x_pt[g].free, x_pt[g].base + 2 * i + 2)
                    transposes(pt[g], [px[:, c // S.MT, (c % S.MT) * P:(c % S.MT + 1) * P]
                                       for c in range(4 * g, 4 * g + 4)], ident).then_inc(x_pt[g].full, 1)
                pe.wait_ge(x_pxt, i + 1)
                for g in range(2):
                    pe.wait_ge(x_pp[g].free, x_pp[g].base + 2 * i + 2)
                    for j in range(4):
                        c = 4 * g + j
                        m = product(pp[g][:, j * P:(j + 1) * P],
                                    [(vm[:, mt, c * P:(c + 1) * P], px_t[:, (c // dc) * S.MT + mt, :])
                                     for mt in range(S.MT)])
                    m.then_inc(x_pp[g].full, 1)

            x_body(0, None)
            with pe.Fori(1, NT) as i:
                x_body(i, i - 1)
            x_out(NT - 1)
            barrier(pe, 5)

            pe.wait_ge(ld["w_r"], 16)
            with pe.Fori(0, NT) as i:
                pe.wait_ge(r_rn.full, i + 1)
                for g in range(2):
                    pe.wait_ge(r_pt[g].free, r_pt[g].base + i + 1)
                    transposes(pt[g], [rn[:, j * P:(j + 1) * P] for j in range(4 * g, 4 * g + 4)], ident)\
                        .then_inc(r_pt[g].full, 1)
                pe.wait_ge(r_rnt, i + 1)
                pe.wait_ge(r_pl.free, i + 1)
                product(pp[0][:, 0:E], [(rn_t[:, k, :], w_r[:, k, :]) for k in range(KD)]).then_inc(r_pl.full, 1)
            pe.wait_ge(r_sel, NT)
            for t in range(NT):
                m = product(pp[1][:, t * E:(t + 1) * E],
                            [(before_b[:, :], sel_b[:, t, :]), (ones_b[:, :], run_b[:, t, :])])
            m.then_inc(r_rank, 1)
            product(wide[0][:, 0:E], [(ones_b[:, :], run_b[:, NT, :])]).then_inc(r_cnt, 1)
            barrier(pe, 6)

            def e_index(i, e):
                pe.wait_ge(e_hot, i + 1)
                for hb in range(2):
                    m = product(wide[1][:, hb * 4:hb * 4 + 4],
                                [(hot[:, t, hb * P:(hb + 1) * P],
                                  mv4[:, t, bass.ds(e, 1), :].rearrange("p o c -> p (o c)")) for t in range(NT)])
                m.then_inc(e_ix, 1)

            def e_turn_in(i):
                pe.wait_ge(e_xg, 32 * (i + 1))
                for g in range(4):
                    b, k = g % 2, g // 2 + 1
                    pe.wait_ge(e_pt[b].free, turn_in_use(b, i, k))
                    transposes(pt[b], [xg[:, j % 2, (2 * g + j // 2) * P:(2 * g + j // 2 + 1) * P] for j in range(4)],
                               ident).then_inc(e_pt[b].full, 1)

            def e_turn_out(i):
                pe.wait_ge(e_yt, i + 1)
                for g in range(4):
                    b, k = g % 2, g // 2 + 1
                    pe.wait_ge(e_pt[b].free, turn_out_use(b, i, k))
                    hb, hd = g // 2, g % 2
                    transposes(pt[b], [y_t[:, 4 * hd + j, hb * P:(hb + 1) * P] for j in range(4)],
                               ident).then_inc(e_pt[b].full, 1)

            SIZES = [128, 160, 192, 224, 256]

            def by_size(rows_, body):
                def pick(sizes):
                    if len(sizes) == 1:
                        body(sizes[0])
                    else:
                        with pe.If(rows_ <= sizes[0]):
                            body(sizes[0])
                        with pe.Else():
                            pick(sizes[1:])
                pick(SIZES)

            def e_gate_up(i, m0, m1, w):
                for m in range(m0, m1):
                    c, b = m // 2, m % 2
                    if m % 2 == 0:
                        pe.wait_ge(e_w[c].full, 16 * (i + 1))
                    pe.wait_ge(e_gu[b].free, e_gu[b].base + 4 * i + m // 2 + 1)
                    for u in range(2):
                        x = product(pp[b][:, u * CAP:u * CAP + w],
                                    [(slots[c][:, k, u * CAP + (m % 2) * P:u * CAP + (m % 2 + 1) * P], xe_t[:, k, 0:w])
                                     for k in range(KD)])
                    x.then_inc(e_gu[b].full, 1)

            def e_down(i, w):
                def act(k):
                    pe.wait_ge(e_act, KD * i + k + 1)
                    return act_t[:, k, 0:w]

                for m in range(KD):
                    c, b = 4 + m // 4, (m // 2) % 2
                    if m % 4 == 0:
                        pe.wait_ge(e_w[c].full, 16 * (i + 1))
                    if m % 2 == 0:
                        pe.wait_ge(e_dn[b].free, 2 * i + m // 4 + 1)
                    x = product(pp2[b][:, (m % 2) * CAP:(m % 2) * CAP + w],
                                ((slots[c][:, k, (m % 4) * P:(m % 4 + 1) * P], act_t[:, k, 0:w] if m else act(k))
                                 for k in range(KD)), KD)
                    if m % 2 == 1:
                        x.then_inc(e_dn[b].full, 1)

            def step(i, before):
                n = pe.value_load(items[0:1, 1, bass.ds(i, 1)], min_val=0, max_val=CAP)
                nxt = pe.value_load(items[0:1, 0, bass.ds(i + 1, 1)], min_val=0, max_val=E - 1)
                pe.wait_ge(e_xt, i + 1)
                by_size(n, lambda w: e_gate_up(i, 0, 2, w))
                e_index(i + 1, nxt)
                if before is not None:
                    e_turn_out(before)
                by_size(n, lambda w: e_gate_up(i, 2, 8, w))
                e_turn_in(i + 1)
                by_size(n, lambda w: e_down(i, w))

            e_index(0, 0)
            e_turn_in(0)
            step(0, None)
            with pe.Fori(1, E) as i:
                step(i, i - 1)
            e_turn_out(E - 1)
            with pe.Fori(E, S.ITEMS) as i:
                active = pe.value_load(items[0:1, 2, bass.ds(i, 1)], min_val=0, max_val=1)
                with pe.If(active > 0):
                    step(i, None)
                    e_turn_out(i)
            barrier(pe, 7)

        @block.vector
        def _(ve):
            def scaled(dst, src, g, k, w):
                return ve.tensor_tensor(dst, src.rearrange("p (k t) -> p k t", k=k),
                                        g.unsqueeze(2).to_broadcast([P, k, w]), ALU.mult)

            for hd in (*m_pt, *m_pp):
                ve.sem_inc(hd.free, 1)
            ve.wait_ge(ld["small"], 64)
            n = 0
            for t in range(S.MT):
                for g in range(KD // 4):
                    b = n % 2
                    ve.wait_ge(m_pt[b].full, n // 2 + 1)
                    scaled(mem_t[:, 4 * g:4 * g + 4, t * P:(t + 1) * P], pt[b][:, :], g_mem[:, 4 * g:4 * g + 4], 4, P)\
                        .then_inc(m_pt[b].free, 1)
                    ve.drain().then_inc(m_rs, 1)
                    n += 1
            n = 0
            for g in range(KD // 2):
                b = n % 2
                ve.wait_ge(m_pp[b].full, n // 2 + 1)
                ve.tensor_copy(km[:, 2 * g:2 * g + 2, :].rearrange("p k t -> p (k t)"), pp[b][:, :])\
                    .then_inc(m_pp[b].free, 1)
                n += 1
            for t in range(S.MT):
                for g in range(D // 512):
                    b = n % 2
                    ve.wait_ge(m_pp[b].full, n // 2 + 1)
                    ve.tensor_copy(vm[:, t, g * 512:(g + 1) * 512], pp[b][:, :]).then_inc(m_pp[b].free, 1)
                    n += 1
            barrier(ve, 1)

            ve.wait_ge(ld["rope"], 32)
            ve.memset(rsum[:, :], 0.0)
            with ve.Fori(0, NT) as i:
                for g in range(2):
                    ve.wait_ge(a_pt[g].full, a_pt[g].base + A_PT[g] * i + 1)
                    scaled(xt[:, 4 * g:4 * g + 4, :], pt[g][:, :], g_mix[:, 4 * g:4 * g + 4], 4, P)\
                        .then_inc(a_pt[g].free, 1)
                ve.drain().then_inc(a_xt, 1)
                ve.sem_inc(a_xn.free, 1)
                ve.wait_ge(a_pp[0].full, a_pp[0].base + 2 * i + 1)
                ve.tensor_copy(lat[:, :], pp[0][:, 0:S.LAT]).then_inc(a_pp[0].free, 1)
                ve.drain()
                ve.tensor_tensor(fz[:, 0, :], lat[:, S.LAT - H:S.LAT], bf_row[:, :], ALU.add)
                ve.drain()
                ve.tensor_scalar(fz[:, 4, :], fz[:, 0, :], -1.0, None, ALU.mult)
                ve.drain()
                ve.tensor_tensor(fz[:, 1, :], fz[:, 0, :], fz[:, 4, :], ALU.min)
                ve.drain().then_inc(a_fz, 1)
                ve.wait_ge(a_lrstd, i + 1)
                ve.tensor_scalar(latn[:, 0:2, :].rearrange("p k c -> p (k c)"), lat[:, 0:S.QR], st_a[:, 6:7], None,
                                 ALU.mult)
                ve.tensor_scalar(latn[:, 2, :], lat[:, S.QR:S.QR + S.KR], st_a[:, 7:8], None, ALU.mult)
                ve.drain().then_inc(a_latn, 1)
                ve.wait_ge(a_fl, i + 1)
                ve.tensor_scalar(fz[:, 4, :], fz[:, 0, :], 0.0, None, ALU.min)
                ve.drain()
                ve.tensor_tensor(fz[:, 5, :], fz[:, 4, :], fz[:, 3, :], ALU.subtract)
                ve.drain().then_inc(a_logf, 1)
                ve.wait_ge(a_pt[0].full, a_pt[0].base + A_PT[0] * i + 2)
                scaled(lat_t[:, :, :], pt[0][:, 0:3 * P], g_lat, 3, P).then_inc(a_pt[0].free, 1)
                ve.drain().then_inc(a_latt, 1)
                ci = cos[:, bass.ds(i, 1), :]
                si = sin[:, bass.ds(i, 1), :]
                hr = S.RO // 2
                kp = lat[:, S.QR + S.KR:S.QR + S.KR + S.RO]
                c1, s1 = ci.rearrange("p o c -> p (o c)"), si.rearrange("p o c -> p (o c)")
                ve.tensor_tensor(krot[:, 0, :], kp, c1, ALU.mult)
                ve.tensor_tensor(krot[:, 1, 0:hr], kp[:, hr:], s1[:, 0:hr], ALU.mult)
                ve.tensor_tensor(krot[:, 1, hr:], kp[:, 0:hr], s1[:, hr:], ALU.mult)
                ve.drain()
                ve.wait_ge(a_up, i + 1)
                ve.tensor_tensor(k_sb[:, :, S.DN:], krot[:, 0:1, :].to_broadcast([P, H, S.RO]),
                                 krot[:, 1:2, :].to_broadcast([P, H, S.RO]), ALU.add)
                qp = q_sb[:, :, S.DN:]
                ve.tensor_tensor(rot[:, 0, :, :], qp, ci.to_broadcast([P, H, S.RO]), ALU.mult)
                ve.tensor_tensor(rot[:, 1, :, 0:hr], qp[:, :, hr:], si[:, :, 0:hr].to_broadcast([P, H, hr]), ALU.mult)
                ve.tensor_tensor(rot[:, 1, :, hr:], qp[:, :, 0:hr], si[:, :, hr:].to_broadcast([P, H, hr]), ALU.mult)
                ve.drain()
                ve.tensor_tensor(qp, rot[:, 0, :, :], rot[:, 1, :, :], ALU.add)
                ve.drain().then_inc(a_qk, 1)
                ve.wait_ge(a_pc.full, i + 1)
                ve.wait_ge(a_st[6].free, 16 * (i + 1))
                ve.tensor_scalar(cneg_sb[:, :], bank_c[0:H, 0:P], -1.0 / SCALE[1], None, ALU.mult)\
                    .then_inc(a_st[6].full, 1)
                ve.tensor_tensor(rsum[:, :], rsum[:, :], fz[:, 5, :], ALU.add)
                ve.drain().then_inc(a_pc.free, 1)
            barrier(ve, 2)

            def row_max(h, n):
                y, i, b = n // NT, n % NT, n % 2
                L = P * (i + 1)
                ve.wait_ge(b_s[b].full, NT * h + n // 2 + 1)
                if y == 0:
                    ve.reduce_max(mx[:, n:n + 1], wide[b][:, 0:L], AX)
                else:
                    if i == 0:
                        ve.wait_ge(b_cneg.full, 16 * (h + 1))
                    apart(ve)
                    ve.tensor_tensor_reduce(biased[b][:, 0:L], wide[b][:, 0:L], cneg[:, 0:L], 1.0, -3e38, ALU.add,
                                            ALU.max, mx[:, n:n + 1]).then_inc(b_s[b].free, 1)
                ve.drain()
                ve.tensor_scalar(nm[:, n:n + 1], mx[:, n:n + 1], -SCALE[y], None, ALU.mult).then_inc(b_nm, 1)
                if n == 2 * NT - 1:
                    ve.drain().then_inc(b_cneg.free, 1)

            with ve.Fori(0, H) as h:
                row_max(h, 0)
                row_max(h, 1)
                for n in range(2 * NT):
                    y, i, b = n // NT, n % NT, n % 2
                    g, tb, k = B_PLAN[n][0]
                    m = min(4, i + 1)
                    ve.wait_ge(b_pt[tb].full, b_pt[tb].base + B_PT[tb] * h + k)
                    ve.tensor_copy(prob_t[b][:, 0:m, :].rearrange("p k t -> p (k t)"), pt[tb][:, 0:m * P])\
                        .then_inc(b_pt[tb].free, 1)
                    ve.drain().then_inc(b_ptd, 1)
                    ve.reciprocal(rr[:, n:n + 1], rs[:, n:n + 1])
                    if n + 2 < 2 * NT:
                        row_max(h, n + 2)
                    ve.drain()
                    ve.wait_ge(b_po[b].full, b_po[b].base + NT * h + n // 2 + 1)
                    ve.tensor_scalar(o_sb[:, i, bass.ds(h * S.DV + y * FW, S.DV)], pp[b][:, 0:S.DV], rr[:, n:n + 1],
                                     None, ALU.mult).then_inc(b_po[b].free, 1)
            barrier(ve, 3)

            with ve.Fori(0, NT) as i:
                for g in range(2):
                    ve.wait_ge(c_pt[g].full, c_pt[g].base + i + 1)
                    scaled(o_t[:, 4 * g:4 * g + 4, :], pt[g][:, :], g_out[:, 4 * g:4 * g + 4], 4, P)\
                        .then_inc(c_pt[g].free, 1)
                ve.drain().then_inc(c_ot, 1)
                ve.sem_inc(c_on.free, 1)
                ve.wait_ge(c_x.full, 16 * (i + 1))
                ht = h_res[:, bass.ds(i, 1), :].rearrange("p o c -> p (o c)")
                for g in range(2):
                    ve.wait_ge(c_pp[g].full, c_pp[g].base + i + 1)
                    cut = slice(g * 512, (g + 1) * 512)
                    ve.tensor_tensor(ht[:, cut], pp[g][:, :], x_again[:, cut], ALU.add).then_inc(c_pp[g].free, 1)
                ve.drain().then_inc(c_x.free, 1)
            barrier(ve, 4)

            def x_residual(i):
                ht = h_res[:, bass.ds(i, 1), :].rearrange("p o c -> p (o c)")
                for g in range(2):
                    ve.wait_ge(x_w[g].full, i + 1)
                    cut = slice(g * 512, (g + 1) * 512)
                    ve.tensor_tensor(ht[:, cut], ht[:, cut], wide[1][:, cut], ALU.add).then_inc(x_w[g].free, 1)

            def x_body(i, before):
                for g in range(2):
                    ve.wait_ge(x_pt[g].full, x_pt[g].base + 2 * i + 1)
                    scaled(hn_t[:, 4 * g:4 * g + 4, :], pt[g][:, :], g_cross[:, 4 * g:4 * g + 4], 4, P)\
                        .then_inc(x_pt[g].free, 1)
                ve.drain().then_inc(x_hnt, 1)
                ve.wait_ge(x_s.full, i + 1)
                ve.tensor_reduce(st_x[:, 4:4 + S.XH], wide[0][:, :].rearrange("p (h m) -> p h m", h=S.XH), AX, ALU.max)
                ve.drain()
                ve.tensor_scalar(st_x[:, 8:8 + S.XH], st_x[:, 4:4 + S.XH], -float(S.XD) ** -0.5, None, ALU.mult)\
                    .then_inc(x_nm, 1)
                ve.wait_ge(x_p, i + 1)
                ve.reciprocal(st_x[:, 16:16 + S.XH], st_x[:, 12:12 + S.XH])
                ve.drain()
                ve.tensor_tensor(px[:, :, :], px[:, :, :],
                                 st_x[:, 16:16 + S.XH].unsqueeze(2).to_broadcast([P, S.XH, S.M]), ALU.mult)\
                    .then_inc(x_pn, 1)
                if before is not None:
                    x_residual(before)
                for g in range(2):
                    ve.wait_ge(x_pt[g].full, x_pt[g].base + 2 * i + 2)
                    ve.tensor_copy(px_t[:, 4 * g:4 * g + 4, :].rearrange("p k t -> p (k t)"), pt[g][:, :])\
                        .then_inc(x_pt[g].free, 1)
                ve.drain().then_inc(x_pxt, 1)

            x_body(0, None)
            with ve.Fori(1, NT) as i:
                x_body(i, i - 1)
            x_residual(NT - 1)
            barrier(ve, 5)

            ve.memset(run_b[:, 0, :], 0.0)
            for j in range(S.TOP):
                ve.memset(jrow[:, j:j + 1], float(j))
            with ve.Fori(0, NT) as i:
                for g in range(2):
                    ve.wait_ge(r_pt[g].full, r_pt[g].base + i + 1)
                    scaled(rn_t[:, 4 * g:4 * g + 4, :], pt[g][:, :], g_ffn[:, 4 * g:4 * g + 4], 4, P)\
                        .then_inc(r_pt[g].free, 1)
                ve.drain().then_inc(r_rnt, 1)
                ve.sem_inc(r_rn.free, 1)
                ve.wait_ge(r_pl.full, i + 1)
                ve.tensor_tensor(lg[:, :], pp[0][:, 0:E], br_row[:, :], ALU.add).then_inc(r_pl.free, 1)
                ve.drain()
                ve.max(val8[:, :], lg[:, :])
                ve.drain()
                ve.tensor_scalar(st_r[:, 4:5], val8[:, 0:1], -1.0, None, ALU.mult)
                ve.max_index(idx8[:, :], val8[:, :], lg[:, :])
                ve.drain().then_inc(r_idx, 1)
                ve.tensor_copy(idxf[:, :], idx8[:, :])
                ve.drain()
                ve.tensor_tensor(eq[:, :, :], iota[:, 0:E].unsqueeze(1).to_broadcast([P, S.TOP, E]),
                                 idxf[:, 0:S.TOP].unsqueeze(2).to_broadcast([P, S.TOP, E]), ALU.is_equal)
                ve.drain()
                ve.tensor_tensor(eqj[:, :, :], eq[:, :, :], jrow[:, :].unsqueeze(2).to_broadcast([P, S.TOP, E]),
                                 ALU.mult)
                sl = sel[:, bass.ds(i, 1), :].rearrange("p o e -> p (o e)")
                sb_ = sel_b[:, bass.ds(i, 1), :].rearrange("p o e -> p (o e)")
                ve.tensor_reduce(sl, eq[:, :, :].rearrange("p j e -> p e j"), AX, ALU.add)
                ve.drain()
                with nc.allow_low_precision(reason="choices 0 to 3 and counts up to 8 are exact in bfloat16"):
                    ve.tensor_reduce(mv4[:, bass.ds(i, 1), :, 2:3].rearrange("p o e c -> p (o e c)"),
                                     eqj[:, :, :].rearrange("p j e -> p e j"), AX, ALU.add)
                ve.tensor_copy(sb_, sl)
                ve.tensor_tensor(run_b[:, bass.ds(i + 1, 1), :].rearrange("p o e -> p (o e)"),
                                 run_b[:, bass.ds(i, 1), :].rearrange("p o e -> p (o e)"), sl, ALU.add)
                ve.drain().then_inc(r_sel, 1)
                ve.wait_ge(r_ex, i + 1)
                ve.reciprocal(st_r[:, 6:7], st_r[:, 5:6])
                ve.drain()
                gt = gates[:, bass.ds(i, 1), :].rearrange("p o c -> p (o c)")
                ve.tensor_scalar(gt, gt, st_r[:, 6:7], None, ALU.mult)
                ve.drain()
            keys = key[:, :, :].rearrange("p t e -> p (t e)")
            ve.wait_ge(r_rank, 1)
            ve.scalar_tensor_tensor(out=keys, in0=pp[1][:, 0:NT * E], scalar=1.0,
                                    in1=sel[:, :, :].rearrange("p t e -> p (t e)"), op0=ALU.add, op1=ALU.mult)
            ve.wait_ge(r_cnt, 1)
            ve.tensor_copy(cnt[:, :], wide[0][:, 0:E])
            ve.drain()
            ve.tensor_scalar(keys, keys, -1.0, None, ALU.add)
            ve.tensor_copy(items[:, 0, 0:E], iota[:, 0:E])
            ve.tensor_scalar(items[:, 1, 0:E], cnt[:, :], float(CAP), None, ALU.min)
            ve.memset(items[:, 2, 0:E], 1)
            ve.memset(shift[:, 0:E], 0.0)
            for b in range(3):
                ve.tensor_scalar(more[:, b, :], cnt[:, :], float(CAP * (b + 1)), None, ALU.is_gt)
            ve.drain()
            ve.tensor_tensor(more[:, 0, :], more[:, 0, :], more[:, 1, :], ALU.add)
            ve.drain()
            ve.tensor_tensor(more[:, 0, :], more[:, 0, :], more[:, 2, :], ALU.add)
            ve.memset(more[:, 1, :], 1.0)
            ve.drain()
            ve.tensor_tensor_scan(more[:, 2, :], more[:, 1, :], more[:, 0, :], 0.0, ALU.mult, ALU.add)
            ve.drain()
            q_row = iota[:, 0:NQ]
            total = more[:, 2, :].unsqueeze(1).to_broadcast([P, NQ, E])
            ve.tensor_tensor(le[:, :, :], total, q_row.unsqueeze(2).to_broadcast([P, NQ, E]), ALU.is_le)
            ve.drain()
            ve.tensor_tensor(le2[:, :, :], le[:, :, :], more[:, 0:1, :].to_broadcast([P, NQ, E]), ALU.mult)
            ve.tensor_reduce(ov[:, 0, :], le[:, :, :], AX, ALU.add)
            ve.drain()
            ve.tensor_reduce(ov[:, 1, :], le2[:, :, :], AX, ALU.add)
            ve.tensor_scalar(ov[:, 2, :], ov[:, 0, :], float(E), None, ALU.is_lt)
            ve.drain()
            ve.tensor_tensor(ov[:, 3, :], q_row, ov[:, 1, :], ALU.subtract)
            ve.tensor_tensor(le[:, :, :], iota[:, 0:E].unsqueeze(1).to_broadcast([P, NQ, E]),
                             ov[:, 0, :].unsqueeze(2).to_broadcast([P, NQ, E]), ALU.is_equal)
            ve.drain()
            ve.tensor_scalar(ov[:, 3, :], ov[:, 3, :], 1.0, float(CAP), ALU.add, ALU.mult)
            ve.tensor_tensor(le2[:, :, :], le[:, :, :], cnt[:, :].unsqueeze(1).to_broadcast([P, NQ, E]), ALU.mult)
            ve.drain()
            ve.tensor_reduce(ov[:, 4, :], le2[:, :, :], AX, ALU.add)
            ve.drain()
            ve.tensor_tensor(ov[:, 4, :], ov[:, 4, :], ov[:, 3, :], ALU.subtract)
            ve.tensor_scalar(shift[:, E:E + NQ], ov[:, 3, :], 0.0, None, ALU.add)
            ve.tensor_scalar(ov[:, 5, :], ov[:, 0, :], float(E - 1), None, ALU.min)
            ve.drain()
            ve.tensor_scalar(ov[:, 4, :], ov[:, 4, :], 0.0, float(CAP), ALU.max, ALU.min)
            ve.tensor_copy(items[:, 0, E:E + NQ], ov[:, 5, :])
            ve.tensor_copy(items[:, 2, E:E + NQ], ov[:, 2, :])
            ve.tensor_scalar(ov[:, 6, :], ov[:, 2, :], -float(8 * T), float(8 * T), ALU.mult, ALU.add)
            ve.drain()
            ve.tensor_copy(items[:, 1, E:E + NQ], ov[:, 4, :])
            ve.tensor_tensor(shift[:, E:E + NQ], shift[:, E:E + NQ], ov[:, 6, :], ALU.add)
            barrier(ve, 6)

            def one_hot(i, e, t):
                return ve.tensor_scalar(hot[:, t, :], iota, shift[:, bass.ds(i, 1)],
                                        key[:, t, bass.ds(e, 1)], ALU.add, ALU.is_equal)

            def indices(i):
                ve.wait_ge(e_ix, i + 1)
                ve.tensor_copy(ix[:, :, :], wide[1][:, 0:8].rearrange("p (h c) -> p h c", h=2))
                ve.drain()
                ve.tensor_tensor(ixt[:, :], ix[:, :, 0], ix[:, :, 1], ALU.add)
                ve.tensor_scalar(ixo[:, :], ix[:, :, 3], -float(8 * T), float(8 * T), ALU.mult, ALU.add)
                ve.drain()
                ve.tensor_tensor(gidx[:, :], ixt[:, :], ixo[:, :], ALU.add)
                ve.scalar_tensor_tensor(out=ixs[:, :], in0=ixt[:, :], scalar=float(S.TOP), in1=ix[:, :, 2],
                                        op0=ALU.mult, op1=ALU.add)
                ve.drain()
                ve.tensor_tensor(ixs[:, :], ixs[:, :], ixo[:, :], ALU.add)
                ve.drain()

            def x_copies(i):
                for g in range(4):
                    b, k = g % 2, g // 2 + 1
                    ve.wait_ge(e_pt[b].full, turn_in_use(b, i, k))
                    scaled(xe_t[:, 2 * g:2 * g + 2, :], pt[b][:, :], g_ffn[:, 2 * g:2 * g + 2], 2, CAP)\
                        .then_inc(e_pt[b].free, 1)
                ve.drain().then_inc(e_xt, 1)

            def step(i, e):
                nxt = ve.value_load(items[0:1, 0, bass.ds(i + 2, 1)], min_val=0, max_val=E - 1)
                for m in range(KD):
                    b = m % 2
                    ve.wait_ge(e_gu[b].full, e_gu[b].base + 4 * i + m // 2 + 1)
                    ve.tensor_scalar(glu[b][:, :], pp[b][:, 0:CAP], b_gu[:, bass.ds(e * 2 * KD + 2 * m, 1)], 7.0,
                                     ALU.add, ALU.min).then_inc(e_glu, 1)
                    ve.tensor_scalar(lin[b][:, :], pp[b][:, CAP:2 * CAP], b_gu[:, bass.ds(e * 2 * KD + 2 * m + 1, 1)],
                                     7.0, ALU.add, ALU.min).then_inc(e_gu[b].free, 1)
                    if m % 2 == 1:
                        ve.sem_inc(e_w[m // 2].free, 1)
                    ve.drain()
                    ve.tensor_scalar(lin[b][:, :], lin[b][:, :], -7.0, 1.0, ALU.max, ALU.add)
                    ve.drain()
                    ve.tensor_tensor(lin[b][:, :], lin[b][:, :], glu[b][:, :], ALU.mult)
                    ve.drain()
                    ve.wait_ge(e_sig, KD * i + m + 1)
                    ve.tensor_tensor(act_t[:, m, :], lin[b][:, :], sig[b][:, :], ALU.mult).then_inc(e_act, 1)
                    if m == 1:
                        indices(i + 1)
                        ve.sem_inc(e_idx, 1)
                    if m == 6:
                        ve.wait_ge(e_left, i + 1)
                        ve.tensor_copy(sidx[:, :], ixp[:, :])
                        ve.drain()
                        ve.tensor_copy(ixp[:, :], ixs[:, :])
                ve.drain()
                x_copies(i + 1)
                hots(i + 2, nxt)

            def hots(i, e):
                for t in range(NT):
                    one_hot(i, e, t)
                ve.drain().then_inc(e_hot, 1)

            hots(0, 0)
            indices(0)
            ve.sem_inc(e_idx, 1)
            ve.tensor_copy(ixp[:, :], ixs[:, :])
            x_copies(0)
            hots(1, 1)
            ve.wait_ge(ld["bias"], 32)
            with ve.Fori(0, E) as i:
                step(i, i)
            with ve.Fori(E, S.ITEMS) as i:
                active = ve.value_load(items[0:1, 2, bass.ds(i, 1)], min_val=0, max_val=1)
                with ve.If(active > 0):
                    e = ve.value_load(items[0:1, 0, bass.ds(i, 1)], min_val=0, max_val=E - 1)
                    step(i, e)
            for b in range(2):
                ve.sem_inc(f_y[b].free, 2)
            barrier(ve, 7)

            ve.wait_ge(ld["g_fin"], 16)
            with ve.Fori(0, NT // 2) as u:
                i = 2 * u
                for b in range(2):
                    ve.wait_ge(f_y[b].full, 8 * i + 16)
                    ht = h_res[:, bass.ds(i + b, 1), :].rearrange("p o c -> p (o c)")
                    for j in range(S.TOP):
                        g = gates[:, bass.ds(i + b, 1), j:j + 1].rearrange("p o c -> p (o c)")
                        ve.scalar_tensor_tensor(out=acc[b][:, :], in0=ye[b][:, j, :], scalar=g,
                                                in1=ht if j == 0 else acc[b][:, :], op0=ALU.mult, op1=ALU.add)
                        if j < S.TOP - 1:
                            ve.drain()
                    ve.drain().then_inc(f_acc, 1)
                    ve.sem_inc(f_y[b].free, 2)
                    ve.wait_ge(f_rstd, i + b + 1)
                    ve.wait_ge(f_out[b], 8 * i + 16)
                    ve.scalar_tensor_tensor(out=of[b][:, :], in0=acc[b][:, :], scalar=st_fin[:, 1:2], in1=g_fin[:, :],
                                            op0=ALU.mult, op1=ALU.mult)
                    ve.drain().then_inc(f_o, 1)


def kernel(**inputs):
    import numpy as _np
    import concourse.bacc as _bacc
    from concourse import mybir as _mybir
    from concourse.bass_utils import run_bass_kernel_spmd as _run

    v = {n: _np.asarray(w) for n, w in inputs.items()}
    S = shapes(v["x"], v["mem"], v["w_q_up"], v["w_router"], v["w_in"])
    C = _np.ascontiguousarray

    def chunks(g):
        return g.reshape(-1, P).T

    at = _np.arange(P)
    const = [_np.eye(P), at[:, None] <= at[None, :], _np.where(at[:, None] < at[None, :], MASKED, 0.0),
             _np.tile(_np.arange(S.CAP), (P, 1)), at[:, None]]
    const = C(_np.concatenate([c.astype(_np.float32) for c in const], axis=1))
    S.NCONST = const.shape[1]
    half = S.RO // 2
    inv = _np.float32(10000.0) ** (-_np.arange(half, dtype=_np.float32) / _np.float32(half))
    angle = _np.arange(S.T, dtype=_np.float32)[:, None] * inv[None, :].astype(_np.float32)
    cos, sin = _np.cos(angle).astype(_np.float32), _np.sin(angle).astype(_np.float32)

    E, KD, D = S.E, S.KD, S.D
    wgu = v["w_gate_up"][0].reshape(E, KD, P, 4, 256, 2).transpose(0, 3, 2, 1, 5, 4).reshape(E * 4, P, KD, 512)
    wdn = v["w_down"][0].reshape(E, KD, P, 2, 512).transpose(0, 3, 2, 1, 4).reshape(E * 2, P, KD, 512)
    bgu = v["b_gate_up"][0].reshape(E, KD, P, 2).transpose(2, 0, 1, 3).reshape(P, E * 2 * KD)
    bdn = v["b_down"][0].reshape(E, KD, P).transpose(2, 0, 1).reshape(P, E * KD)
    gains = _np.concatenate([chunks(v["ln_mix"][0]), chunks(v["ln_cross"][0]), chunks(v["mem_norm"][0]),
                             chunks(v["ln_ffn"][0]), chunks(v["q_norm"][0]), chunks(v["kv_norm"][0]),
                             chunks(v["g_out_mla"][0]), chunks(v["g_out_fox"][0])], axis=1)
    feed = {
        "const": const, "cos": C(_np.concatenate([cos, cos], 1)), "sin": C(_np.concatenate([-sin, sin], 1)),
        "gains": C(gains), "w_gu": C(wgu), "w_dn": C(wdn), "b_gu": C(bgu), "b_dn": C(bdn),
    }
    for n in ("x", "mem", "w_in", "w_q_up", "w_kv_up", "b_forget", "w_o", "w_xq", "w_mem_kv", "w_xo", "w_router",
              "b_router", "ln_final"):
        feed[n] = C(v[n])

    nc = _bacc.Bacc("TRN2", target_bir_lowering=False, num_devices=1)
    arrays = {f"in_{n}": w for n, w in feed.items()}
    a = {n: nc.dram_tensor(f"in_{n}", w.shape, _mybir.dt.from_np(w.dtype), kind="ExternalInput").ap()
         for n, w in feed.items()}
    out = nc.dram_tensor("out_h", v["x"].shape, F32, kind="ExternalOutput").ap()
    build(nc, S, a, out)
    r = _run(nc, [arrays], core_ids=[0])
    return r.results[0]["out_h"]
```

```python
from contextlib import ExitStack

import concourse.bass as bass
import numpy as np
from concourse import mybir

F32 = mybir.dt.float32
BF16 = mybir.dt.bfloat16
I32 = mybir.dt.int32
U32 = mybir.dt.uint32
ALU = mybir.AluOpType
ACT = mybir.ActivationFunctionType
AX = mybir.AxisListType.X

P = 128
EPS = 1e-6
MASKED = -1e30


class Handoff:

    def __init__(self, sem, name):
        self.full = sem(name + "_full")
        self.free = sem(name + "_free")
        self.base = 0

    def after(self, fills):
        later = object.__new__(Handoff)
        later.full, later.free, later.base = self.full, self.free, self.base + fills
        return later


def shapes(x, mem, w_q_up, w_router, w_in):
    class S:
        pass

    S.T, S.D = x.shape[1:]
    S.NT, S.KD = S.T // P, S.D // P
    S.M = mem.shape[1]
    S.MT = S.M // P
    S.QR, S.KR, S.RO = 256, 128, 32
    S.H, S.DN, S.DV = 8, 64, 64
    S.DQ = S.DN + S.RO
    S.FW = S.H * S.DV
    S.LAT = S.QR + S.KR + S.RO + S.H
    S.IN = S.LAT + 3 * S.FW
    S.XH, S.XD = 4, S.D // 4
    S.E = w_router.shape[-1]
    S.TOP = 4
    S.CAP = 256
    S.MORE = S.T * S.TOP // (S.CAP + 1)
    S.ITEMS = S.E + S.MORE
    return S


def build(nc, S, a, out):
    T, D, NT, KD, H, FW, E, CAP = S.T, S.D, S.NT, S.KD, S.H, S.FW, S.E, S.CAP
    ctx = ExitStack()
    with ctx:
        def sem(name):
            return ctx.enter_context(nc.semaphore(name))

        base = (nc.sbuf_base + 63) // 64 * 64

        class Region:

            def __init__(self, start, end):
                self.at, self.end = base + int(start * 1024), base + int(end * 1024)

            def __call__(self, name, shape, dt=F32):
                t = nc.alloc_sbuf_tensor_at(name, shape, dt, offset=self.at)
                size = int(np.prod(shape[1:])) * (2 if dt == BF16 else 4)
                self.at += (size + 63) // 64 * 64
                assert self.at <= self.end, (name, (self.at - base) / 1024)
                return t

        keep = Region(0, 15)
        const = keep("const", [P, S.NCONST])
        ident, tri, mask = const[:, 0:P], const[:, P:2 * P], const[:, 2 * P:3 * P]
        iota = const[:, 3 * P:3 * P + CAP]
        pcol = const[:, 3 * P + CAP:3 * P + CAP + 1]
        ident_b = keep("ident_b", [P, P], BF16)
        mask_b = keep("mask_b", [P, P], BF16)
        before_b = keep("before_b", [P, P], BF16)
        ones_b = keep("ones_b", [P, P], BF16)
        ones = keep("ones", [P, P])
        gains = keep("gains", [P, 4 * KD + 3 + KD])
        g_mix, g_cross, g_mem, g_ffn = (gains[:, k * KD:(k + 1) * KD] for k in range(4))
        g_lat, g_out = gains[:, 4 * KD:4 * KD + 3], gains[:, 4 * KD + 3:]
        bf_row = keep("bf_row", [P, H])
        br_row = keep("br_row", [P, E])
        gates = keep("gates", [P, NT, S.TOP])
        key = keep("key", [P, NT, E])
        mv = keep("mv", [P, NT * E * 4], BF16)
        mv4 = mv[:, :].rearrange("p (t e c) -> p t e c", t=NT, e=E)
        shift = keep("shift", [P, S.ITEMS + 2])
        items = keep("items", [P, 3, S.ITEMS + 2], I32)
        half = keep("half", [P, 16])
        sums = keep("sums", [P, 32])
        rstd = keep("rstd", [P, 32])
        CN, XN, RN = 0, 16, 24
        w_r = keep("w_r", [P, KD, E])
        rn_t = keep("rn_t", [P, KD, P])
        lg = keep("lg", [P, NT, E])
        xscale = keep("xscale", [P, NT])
        h_res = Region(15, 47)("h_res", [P, NT, D])
        km = Region(47, 55)("km", [P, KD, S.M])
        vm = Region(55, 63)("vm", [P, S.MT, D])
        w_mem_k = Region(15, 47)("w_mem_k", [P, KD, D])
        w_mem_v = Region(95, 127)("w_mem_v", [P, KD, D])
        r = Region(63, 95)
        mem_sb = r("mem_sb", [P, S.MT, D])
        mem_n = r("mem_n", [P, S.MT, D])
        mem_t = r("mem_t", [P, KD, S.M])
        mem_ss = r("mem_ss", [P, 4])
        r = Region(63, 95)
        v_mla = r("v_mla", [P, NT, FW])
        v_fox = r("v_fox", [P, NT, FW])
        r = Region(134, 207)
        w_in = r("w_in", [P, KD, S.IN])
        w_qu = r("w_qu", [P, 2, H * S.DQ])
        w_ku = r("w_ku", [P, H * 2 * S.DN])
        r = Region(15, 47)
        x_sb = Region(130, 134)("x_sb", [P, D])
        xt = r("xt", [P, KD, P])
        sq_a = r("sq_a", [P, D])
        lat = r("lat", [P, S.LAT])
        latn = r("latn", [P, 3, P])
        lat_t = r("lat_t", [P, 3, P])
        cos = r("cos", [P, NT, S.RO])
        sin = r("sin", [P, NT, S.RO])
        st_a = r("st_a", [P, 16])
        rstd_a = r("rstd_a", [P, NT])
        fz = r("fz", [P, 6, H])
        rsum = r("rsum", [P, H])
        assert S.RO == 32
        r = Region(95, 130)
        fq_sb = r("fq_sb", [P, FW])
        fk_sb = r("fk_sb", [P, FW])
        q_sb = r("q_sb", [P, H, S.DQ])
        k_sb = r("k_sb", [P, H, S.DQ])
        rot = r("rot", [P, 2, H, S.RO])
        krot = r("krot", [P, 2, S.RO])
        st_q = [r(f"st_q{g}", [S.DQ, 4, P]) for g in range(4)]
        st_f = [r(f"st_f{g}", [P, 4, P]) for g in range(2)]
        cneg_sb = r("cneg_sb", [H, P])
        w_o = Region(95, 127)("w_o", [P, KD, D])
        o_sb = Region(127, 159)("o_sb", [P, NT, D])
        r = Region(15, 47)
        prob = [r(f"prob{b}", [P, T]) for b in range(2)]
        prob_t = [r(f"prob_t{b}", [P, NT, P]) for b in range(2)]
        biased = [r(f"biased{b}", [P, T]) for b in range(2)]
        cneg = r("cneg", [P, T])
        mx = r("mx", [P, 16])
        nm = r("nm", [P, 16])
        rs = r("rs", [P, 16])
        rr = r("rr", [P, 16])
        r = Region(159, 175)
        qt = [r("qt_mla", [S.DQ, T]), r("qt_fox", [S.DN, T])]
        kt = [r("kt_mla", [S.DQ, T]), r("kt_fox", [S.DN, T])]
        w_xq = Region(175, 207)("w_xq", [P, KD, D])
        r = Region(159, 175)
        x_again = r("x_again", [P, D])
        o_t = [r(f"o_t{b}", [P, KD, P]) for b in range(2)]
        assert r.at <= base + 171 * 1024
        row = Region(171, 175)("row", [P, D])
        w_xo = Region(63, 95)("w_xo", [P, KD, D])
        r = Region(143, 171)
        hn_t = r("hn_t", [P, KD, P])
        qx_t = r("qx_t", [P, KD, P])
        px = r("px", [P, S.XH, S.M])
        px_t = r("px_t", [P, KD, P])
        ox_t = r("ox_t", [P, KD, P])
        sq_c = r("sq_c", [P, D])
        st_x = r("st_x", [P, 32])
        r = Region(143, 171)
        rn_places = [Region(63, 87), Region(159, 167)]
        rn = [rn_places[t // 6](f"rn{t}", [P, D]) for t in range(NT)]
        val8 = r("val8", [P, NT, 8])
        idx8 = r("idx8", [P, NT, 8], U32)
        idxf = r("idxf", [P, NT, 8])
        gate_sum = r("gate_sum", [P, NT])
        eq = r("eq", [P, NT, S.TOP, E])
        eqj = r("eqj", [P, NT, S.TOP, E])
        jrow = r("jrow", [P, S.TOP])
        sel = r("sel", [P, NT, E])
        sel_b = r("sel_b", [P, NT, E], BF16)
        run_b = r("run_b", [P, NT + 1, E], BF16)
        r = Region(191, 207)
        cnt = r("cnt", [P, E])
        more = r("more", [P, 4, E])
        NQ = S.MORE + 2
        le = r("le", [P, NQ, E])
        le2 = r("le2", [P, NQ, E])
        ov = r("ov", [P, 8, NQ])
        SLOTS = 6
        slots = [Region(95 + 16 * c, 111 + 16 * c)(f"slot{c}", [P, KD, 512]) for c in range(SLOTS)]
        r = Region(63, 95)
        act_t = r("act_t", [P, KD, CAP])
        y_t = r("y_t", [P, KD, CAP])
        y_sb = r("y_sb", [P, 2, D])
        xg = r("xg", [P, 2, D])
        r = Region(47, 63)
        xe_t = r("xe_t", [P, KD, CAP])
        hot = r("hot", [P, NT, CAP], BF16)
        r = Region(191, 207)
        b_gu = r("b_gu", [P, E * 2 * KD])
        b_dn = r("b_dn", [P, E * KD])
        glu = [r(f"glu{b}", [P, CAP]) for b in range(2)]
        lin = [r(f"lin{b}", [P, CAP]) for b in range(2)]
        sig = [r(f"sig{b}", [P, CAP]) for b in range(2)]
        ix = r("ix", [P, 2, 4])
        ixt = r("ixt", [P, 2])
        ixo = r("ixo", [P, 2])
        ixs = r("ixs", [P, 2])
        ixp = r("ixp", [P, 2])
        gidx = r("gidx", [P, 2], I32)
        sidx = r("sidx", [P, 2], I32)
        r = Region(95, 207)
        ye = [r(f"ye{b}", [P, S.TOP, D]) for b in range(2)]
        acc = [r(f"acc{b}", [P, D]) for b in range(2)]
        sq_f = r("sq_f", [P, D])
        g_fin = r("g_fin", [P, D])
        of = [r(f"of{b}", [P, D]) for b in range(2)]
        sum_f = r("sum_f", [P, 2])
        rstd_f = r("rstd_f", [P, 2])

        def scratch(name, shape, dt=F32):
            return nc.dram_tensor(name, shape, dt, kind="Internal").ap()

        d_q = scratch("d_q", [H, S.DQ, T])
        d_k = scratch("d_k", [H, S.DQ, T])
        d_fq = scratch("d_fq", [FW, T])
        d_fk = scratch("d_fk", [FW, T])
        d_cneg = scratch("d_cneg", [H, T])
        d_xn = scratch("d_xn", [T, D])
        d_y = scratch("d_y", [T * S.TOP, D])

        bank = [ctx.enter_context(nc.psum_tensor(f"bank{b}", [P, 512], F32)) for b in range(4)]
        wide = [ctx.enter_context(nc.psum_tensor(f"wide{b}", [P, 1024], F32)) for b in range(2)]
        pt = bank[0:2]
        pp = bank[2:4]

        def bank_u(g):
            return wide[0][:, g * 512:(g + 1) * 512]

        bank_c = wide[1]
        pp2 = [wide[0][:, 0:512], wide[0][:, 512:1024]]
        SCALE = [float(S.DQ) ** -0.5, float(S.DN) ** -0.5]
        A_ST = [(1, 2, S.DQ), (0, 3, S.DQ), (1, 3, S.DQ), (0, 4, S.DQ), (1, 4, P), (0, 5, P)]
        A_PT = [5, 4]

        def a_in_use(b, i):
            return a_pt[b].base + (1 if isinstance(i, int) and i == 0 else A_PT[b] * i - 2)

        def a_st_use(b, i, k, more):
            return a_pt[b].base + A_PT[b] * i + k + (1 if more else 0)


        long_short = [i for k in range(NT // 2) for i in (NT - 1 - k, k)]
        B_STEPS = [(0, i) for i in long_short] + [(1, i) for i in long_short]
        B_FIRST, B_LAST = (0, NT), (NT - 1, 2 * NT - 1)

        def b_groups():
            used, plan = [0, 0], []
            for n in range(2 * NT):
                mine = []
                for g in range(B_STEPS[n][1] // 4 + 1):
                    b = (n + g) % 2
                    used[b] += 1
                    mine.append((g, b, used[b]))
                plan.append(mine)
            return plan, used

        def b_ahead(h, n, last):
            if n < 2 * NT:
                return h, n
            return None if last else (h + 1, n - 2 * NT)

        def b_loop(eng, body):
            with eng.Fori(0, H - 1) as h:
                body(h, False)
            body(H - 1, True)

        B_PLAN, B_PT = b_groups()
        B_GRP1 = sum(len(g) > 1 for g in B_PLAN)

        ld = {n: sem("ld_" + n) for n in (
            "small", "mem", "w_mem_k", "w_mem_v", "w_in", "rope", "w_o", "w_xq", "w_xo",
            "w_r", "bias", "g_fin")}
        stage_end, passed = sem("stage_end"), sem("passed")
        init = sem("init")

        ENGINES = 5

        def barrier(eng, n):
            eng.drain().then_inc(stage_end, 1)
            eng.wait_ge(stage_end, ENGINES * n)

        m_ss, m_rs, m_n = sem("m_ss"), sem("m_rs"), sem("m_n")
        m_pt = [Handoff(sem, f"pt{b}") for b in range(2)]
        m_pp = [Handoff(sem, f"pp{b}") for b in range(2)]
        a_pt = [m_pt[b].after(S.MT * KD // 8) for b in range(2)]
        a_pp = [m_pp[b].after((KD // 2 + S.MT * D // 512) // 2) for b in range(2)]
        b_pt = [a_pt[b].after(A_PT[b] * NT) for b in range(2)]
        b_po = [a_pp[b].after(2 * NT) for b in range(2)]
        c_pt = [b_pt[b].after(B_PT[b] * H) for b in range(2)]
        c_pp = [b_po[b].after(NT * H) for b in range(2)]
        x_pt = [c_pt[b].after(NT) for b in range(2)]
        x_pp = [c_pp[b].after(NT) for b in range(2)]
        e_pt = [x_pt[b].after(3 * NT) for b in range(2)]

        def turn_in_use(b, i, k):
            return e_pt[b].base + k if isinstance(i, int) and i == 0 else e_pt[b].base + 4 * i - 2 + k

        def turn_out_use(b, i, k):
            return e_pt[b].base + 4 * i + 4 + k

        e_gu = [x_pp[b].after(2 * NT) for b in range(2)]

        a_x = Handoff(sem, "a_x")
        a_ss, a_rstd, a_lss, a_lrstd = sem("a_ss"), sem("a_rstd"), sem("a_lss"), sem("a_lrstd")
        a_xt, a_latn, a_latt = sem("a_xt"), sem("a_latn"), sem("a_latt")
        a_pu = [Handoff(sem, f"a_pu{b}") for b in range(2)]
        a_pc = Handoff(sem, "a_pc")
        a_fz, a_fl, a_logf = sem("a_fz"), sem("a_fl"), sem("a_logf")
        a_up, a_qk = sem("a_up"), sem("a_qk")
        a_st = [Handoff(sem, f"a_st{g}") for g in range(7)]

        b_in = [Handoff(sem, f"b_in{y}") for y in range(2)]
        b_cneg = Handoff(sem, "b_cneg")
        b_s = [Handoff(sem, f"b_s{b}") for b in range(2)]
        b_nm = sem("b_nm")
        b_p = [Handoff(sem, f"b_p{b}") for b in range(2)]
        b_ptd, b_pta = sem("b_ptd"), sem("b_pta")

        c_ss, c_rstd, c_ot, c_h = sem("c_ss"), sem("c_rstd"), sem("c_ot"), sem("c_h")
        c_x = Handoff(sem, "c_x")
        c_row = Handoff(sem, "row")
        x_row = c_row.after(NT)
        c_w = [Handoff(sem, f"c_w{b}") for b in range(2)]

        x_rstd, x_hnt, x_qx, x_h = sem("x_rstd"), sem("x_hnt"), sem("x_qx"), sem("x_h")
        x_s = Handoff(sem, "x_s")
        x_nm, x_p, x_pn, x_pxt, x_ox = sem("x_nm"), sem("x_p"), sem("x_pn"), sem("x_pxt"), sem("x_ox")
        x_w = [Handoff(sem, f"x_w{b}") for b in range(2)]

        x_order = [("T", 0)]
        for t in range(NT):
            x_order += [("T", t + 1)] * (t + 1 < NT) + [("O", t - 1)] * (t >= 1) + [("R", t - 2)] * (t >= 2)
            x_order += [("P", t)] + [("L", t - 2)] * (t >= 2)
        x_order += [("O", NT - 1), ("R", NT - 2), ("L", NT - 2), ("R", NT - 1), ("L", NT - 1)]

        def x_use(kinds, kind, i):
            places = [x for x in x_order if x[0] in kinds]
            if isinstance(i, int):
                return places.index((kind, i)) + 1
            first, second = (places.index((kind, t)) + 1 for t in (3, 4))
            return first - 3 * (second - first) + (second - first) * i

        def x_pt_use(b, kind, i):
            return x_pt[b].base + x_use("TPR", kind, i)

        def x_row_use(kind, i):
            return x_row.base + x_use("TR", kind, i)

        def x_w_use(g, kind, i):
            return x_use("OL" if g == 0 else "O", kind, i)

        def pairs(eng, body):
            with eng.Fori(0, NT // 2 - 1) as u:
                body(2 * u, 0, True)
                body(2 * u + 1, 1, True)
            body(NT - 2, 0, True)
            body(NT - 1, 1, False)

        def further_blocks(eng, body):
            some = eng.value_load(items[0:1, 2, E:E + 1], min_val=0, max_val=1)
            with eng.If(some > 0):
                with eng.Fori(E, S.ITEMS) as i:
                    active = eng.value_load(items[0:1, 2, bass.ds(i, 1)], min_val=0, max_val=1)
                    with eng.If(active > 0):
                        body(i)

        r_rstd, r_rnt, r_idx, r_ex, r_sel, r_rn = (
            sem("r_rstd"), sem("r_rnt"), sem("r_idx"), sem("r_ex"), sem("r_sel"), sem("r_rn"))
        r_st = sem("r_st")
        r_rank = sem("r_rank")
        r_cnt = sem("r_cnt")

        e_w = [Handoff(sem, f"e_w{c}") for c in range(SLOTS)]
        e_hot, e_ix = sem("e_hot"), sem("e_ix")
        e_idx = sem("e_idx")
        e_xg = sem("e_xg")
        e_y = Handoff(sem, "e_y")
        e_left = sem("e_left")
        e_dn = [Handoff(sem, f"e_dn{b}") for b in range(2)]
        e_xt, e_glu, e_sig, e_act, e_yt = sem("e_xt"), sem("e_glu"), sem("e_sig"), sem("e_act"), sem("e_yt")

        f_y = [Handoff(sem, f"f_y{b}") for b in range(2)]
        f_acc, f_ss, f_rstd, f_o = sem("f_acc"), sem("f_ss"), sem("f_rstd"), sem("f_o")
        f_out = [sem(f"f_out{b}") for b in range(2)]

        def apart(eng):
            eng.sem_inc(passed, 1)

        block = ctx.enter_context(nc.Block())

        def rows(w):
            return w.rearrange("(k p) n -> p k n", p=P)

        @block.sync
        def _(sp):
            def load(dst, src, s):
                sp.dma_start(dst, src).then_inc(s, 16)

            load(mem_sb[:, :, :], a["mem"][0].rearrange("(t p) d -> p t d", p=P), ld["mem"])
            load(const[:, :], a["const"], ld["small"])
            load(gains[:, :], a["gains"], ld["small"])
            load(bf_row[:, :], a["b_forget"][0].partition_broadcast(P), ld["small"])
            load(br_row[:, :], a["b_router"][0].partition_broadcast(P), ld["small"])
            load(w_mem_k[:, :, :], rows(a["w_mem_kv"][0])[:, :, 0:D], ld["w_mem_k"])
            load(w_mem_v[:, :, :], rows(a["w_mem_kv"][0])[:, :, D:2 * D], ld["w_mem_v"])
            w = rows(a["w_in"][0])
            cut = S.LAT - H
            load(w_in[:, :, 0:cut], w[:, :, 0:cut], ld["w_in"])
            load(w_in[:, :, cut:S.LAT], w[:, :, S.IN - H:S.IN], ld["w_in"])
            load(w_in[:, :, S.LAT:S.IN], w[:, :, cut:S.IN - H], ld["w_in"])
            load(w_qu[:, :, :], rows(a["w_q_up"][0]), ld["w_in"])
            load(w_ku[:, :], a["w_kv_up"][0], ld["w_in"])
            load(x_sb[:, :], a["x"][0, 0:P, :], a_x.full)
            barrier(sp, 1)

            load(cos[:, :, :], a["cos"].rearrange("(t p) c -> p t c", p=P), ld["rope"])
            load(sin[:, :, :], a["sin"].rearrange("(t p) c -> p t c", p=P), ld["rope"])
            def load_x(i):
                sp.wait_ge(a_x.free, 2 * i)
                load(x_sb[:, :], a["x"][0, bass.ds(i * P, P), :], a_x.full)

            def store_qk(i):
                for g in range(4):
                    dst = (d_q, d_k)[g // 2]
                    h0 = 4 * (g % 2)
                    sp.wait_ge(a_st[g].full, i + 1)
                    sp.dma_start(dst[h0:h0 + 4, :, bass.ds(i * P, P)].rearrange("h d t -> d h t"),
                                 st_q[g][:, :, :]).then_inc(a_st[g].free, 16)
                for g in range(2):
                    dst = (d_fq, d_fk)[g]
                    sp.wait_ge(a_st[4 + g].full, i + 1)
                    sp.dma_start(dst[:, bass.ds(i * P, P)].rearrange("(c p) t -> p c t", p=P),
                                 st_f[g][:, :, :]).then_inc(a_st[4 + g].free, 16)
                sp.wait_ge(a_st[6].full, i + 1)
                sp.dma_start(d_cneg[:, bass.ds(i * P, P)], cneg_sb[:, :]).then_inc(a_st[6].free, 16)

            with sp.Fori(0, NT - 1) as i:
                load_x(i + 1)
                store_qk(i)
            store_qk(NT - 1)
            for g in range(7):
                sp.wait_ge(a_st[g].free, 16 * (NT + 1))
            barrier(sp, 2)

            def load_heads(h):
                for y in range(2):
                    sp.wait_ge(b_in[y].free, h + 1)
                    src = ((d_q, d_k), (d_fq, d_fk))[y]
                    for dst, s in zip((qt[y], kt[y]), src):
                        s = s[bass.ds(h, 1), :, :].rearrange("h d t -> (h d) t") if y == 0 \
                            else s[bass.ds(h * S.DN, S.DN), :]
                        load(dst[:, :], s, b_in[y].full)
                sp.wait_ge(b_cneg.free, h + 1)
                load(cneg[:, :], d_cneg[bass.ds(h, 1), :].to_broadcast([P, T]), b_cneg.full)

            load_heads(0)
            load(w_o[:, :, :], rows(a["w_o"][0]), ld["w_o"])
            with sp.Fori(1, H) as h:
                load_heads(h)
            load(w_xq[:, :, :], rows(a["w_xq"][0]), ld["w_xq"])
            barrier(sp, 3)

            load(w_xo[:, :, :], rows(a["w_xo"][0]), ld["w_xo"])
            load(w_r[:, :, :], rows(a["w_router"][0]), ld["w_r"])
            with sp.Fori(0, NT) as i:
                sp.wait_ge(c_x.free, i + 1)
                load(x_again[:, :], a["x"][0, bass.ds(i * P, P), :], c_x.full)
            barrier(sp, 4)

            def expert_part(c, e):
                if c < 4:
                    return a["w_gu"][bass.ds(e * 4 + c, 1), :, :, :].rearrange("a p k n -> (a p) k n")
                return a["w_dn"][bass.ds(e * 2 + c - 4, 1), :, :, :].rearrange("a p k n -> (a p) k n")

            for c in range(3):
                load(slots[c][:, :, :], expert_part(c, 0), e_w[c].full)
            barrier(sp, 5)

            for t in range(NT):
                sp.wait_ge(r_rn, t + 1)
                sp.dma_start(d_xn[t * P:(t + 1) * P, :], rn[t][:, :]).then_inc(r_st, 16)
            sp.wait_ge(r_st, 16 * NT)
            barrier(sp, 6)

            load(b_gu[:, :], a["b_gu"], ld["bias"])
            load(b_dn[:, :], a["b_dn"], ld["bias"])
            sp.wait_ge(e_xg, 32)
            for c in range(3, SLOTS):
                load(slots[c][:, :, :], expert_part(c, 0), e_w[c].full)

            def refill(i, e):
                for c in range(SLOTS):
                    sp.wait_ge(e_w[c].free, i)
                    load(slots[c][:, :, :], expert_part(c, e), e_w[c].full)

            with sp.Fori(1, E) as i:
                refill(i, i)

            def sp_further(i):
                e = sp.value_load(items[0:1, 0, bass.ds(i, 1)], min_val=0, max_val=E - 1)
                refill(i, e)

            further_blocks(sp, sp_further)
            barrier(sp, 7)

            load(g_fin[:, :], a["ln_final"].partition_broadcast(P), ld["g_fin"])
            yt = d_y.rearrange("(i p c) d -> i p c d", p=P, c=S.TOP)
            with sp.Fori(0, NT // 2) as u:
                i = 2 * u
                for b in range(2):
                    sp.wait_ge(f_y[b].free, i + 2)
                    load(ye[b][:, :, :], yt[bass.ds(i + b, 1), :, :, :].rearrange("i p c d -> (i p) c d"),
                         f_y[b].full)

        @block.gpsimd
        def _(po):
            po.memset(half[:, :], -0.5).then_inc(init, 1)

            def power(dst, src, n, k):
                po.tensor_scalar(dst, src, 1.0 / n, EPS, ALU.mult, ALU.add)
                po.drain()
                return po.tensor_tensor(dst, dst, half[:, 0:k], ALU.pow)

            po.wait_ge(m_ss, S.MT)
            power(mem_ss[:, 2:2 + S.MT], mem_ss[:, 0:S.MT], D, S.MT).then_inc(m_rs, 1)
            po.memset(ones[:, :], 1.0).then_inc(init, 1)
            po.memset(ones_b[:, :], 1.0).then_inc(init, 1)
            po.memset(mv[:, :], 1.0)
            po.drain()
            for t in range(NT):
                po.memset(mv4[:, t, :, 1], float(P * t))
            po.wait_ge(ld["small"], 64)
            po.tensor_copy(mv[:, :].rearrange("p (n c) -> p n c", c=4)[:, :, 0], pcol.to_broadcast([P, NT * E]))
            po.tensor_copy(ident_b[:, :], ident).then_inc(init, 1)
            po.tensor_copy(mask_b[:, :], mask).then_inc(init, 1)
            po.tensor_tensor(before_b[:, :], tri, ident, ALU.subtract).then_inc(init, 1)
            barrier(po, 1)

            def a_latent(i):
                po.wait_ge(a_lss, i + 1)
                apart(po)
                power(st_a[:, 6:7], st_a[:, 2:3], S.QR, 1)
                power(st_a[:, 7:8], st_a[:, 3:4], S.KR, 1).then_inc(a_lrstd, 1)

            def a_pre(i):
                po.wait_ge(a_ss, i + 1)
                apart(po)
                power(st_a[:, 4:5], st_a[:, 0:1], D, 1)
                po.drain()
                po.tensor_copy(rstd_a[:, bass.ds(i, 1)], st_a[:, 4:5]).then_inc(a_rstd, 1)

            a_pre(0)
            with po.Fori(0, NT - 1) as i:
                a_latent(i)
                a_pre(i + 1)
            a_latent(NT - 1)
            barrier(po, 2)
            barrier(po, 3)

            def rows_of(src, hd, i, use):
                po.wait_ge(hd.free, use)
                apart(po)
                po.tensor_copy(row[:, :], src[:, bass.ds(i, 1), :].rearrange("p o c -> p (o c)")).then_inc(hd.full, 1)

            po.sem_inc(c_row.free, 1)
            rows_of(o_sb, c_row, 0, 1)
            rows_of(o_sb, c_row, 1, 2)
            po.wait_ge(c_ss, 1)
            power(rstd[:, CN:CN + 2 * NT], sums[:, CN:CN + 2 * NT], FW, 2 * NT).then_inc(c_rstd, 1)
            with po.Fori(2, NT) as i:
                rows_of(o_sb, c_row, i, i + 1)
            barrier(po, 4)

            def x_rows(i):
                rows_of(h_res, x_row, i, x_row_use("T", i))

            x_rows(0)
            power(rstd[:, XN:XN + NT], sums[:, XN:XN + NT], D, NT)
            po.drain()
            po.tensor_scalar(xscale[:, :], rstd[:, XN:XN + NT], float(S.XD) ** -0.5, None, ALU.mult)\
                .then_inc(x_rstd, 1)

            def r_rows(i):
                po.wait_ge(x_h, i + 1)
                rows_of(h_res, x_row, i, x_row_use("R", i))

            x_rows(1)
            x_rows(2)
            with po.Fori(2, NT - 1) as i:
                x_rows(i + 1)
                r_rows(i - 2)
            for t in range(NT - 3, NT):
                r_rows(t)
            barrier(po, 5)
            power(rstd[:, RN:RN + NT], sums[:, RN:RN + NT], D, NT).then_inc(r_rstd, 1)
            po.memset(xg[:, :, :], 0.0)
            po.drain()

            def gather(i):
                po.wait_ge(e_idx, i + 1)
                apart(po)
                for hb in range(2):
                    po.indirect_dma_start(
                        out=xg[:, hb, :], out_offset=None, in_=d_xn,
                        in_offset=bass.IndirectOffsetOnAxis(ap=gidx[:, hb:hb + 1], axis=0),
                        bounds_check=T - 1, oob_is_err=False).then_inc(e_xg, 16)

            po.wait_ge(r_st, 16 * NT)
            gather(0)
            barrier(po, 6)

            def scatter(i):
                po.wait_ge(e_y.full, i + 1)
                apart(po)
                for hb in range(2):
                    po.indirect_dma_start(
                        out=d_y, out_offset=bass.IndirectOffsetOnAxis(ap=sidx[:, hb:hb + 1], axis=0),
                        in_=y_sb[:, hb, :], in_offset=None,
                        bounds_check=T * S.TOP - 1, oob_is_err=False).then_inc(e_y.free, 16)
                po.wait_ge(e_y.free, 32 * (i + 1))
                po.sem_inc(e_left, 1)

            po.sem_inc(e_left, 1)
            gather(1)
            with po.Fori(1, E) as i:
                gather(i + 1)
                scatter(i - 1)
            scatter(E - 1)

            def po_further(i):
                gather(i + 1)
                scatter(i)

            further_blocks(po, po_further)
            po.sem_inc(f_out[0], 16)
            po.sem_inc(f_out[1], 16)
            barrier(po, 7)
            with po.Fori(0, NT // 2) as u:
                for b in range(2):
                    po.wait_ge(f_ss, 2 * u + b + 1)
                    apart(po)
                    power(rstd_f[:, b:b + 1], sum_f[:, b:b + 1], D, 1).then_inc(f_rstd, 1)

        @block.scalar
        def _(ac):
            ac.wait_ge(ld["mem"], 16)
            for t in range(S.MT):
                ac.activation(mem_n[:, t, :], mem_sb[:, t, :], ACT.Square, accum_out=mem_ss[:, t:t + 1])
                ac.drain().then_inc(m_ss, 1)
            ac.wait_ge(m_rs, 1)
            for t in range(S.MT):
                ac.activation(mem_n[:, t, :], mem_sb[:, t, :], ACT.Copy, scale=mem_ss[:, 2 + t:3 + t]).then_inc(m_n, 1)
            barrier(ac, 1)

            for g in range(7):
                ac.sem_inc(a_st[g].free, 16)
            for hd in (a_pc, *a_pu):
                ac.sem_inc(hd.free, 1)

            def a_pre(i):
                ac.wait_ge(a_x.full, 16 * (i + 1))
                ac.activation(sq_a[:, :], x_sb[:, :], ACT.Square, accum_out=st_a[:, 0:1])
                ac.drain().then_inc(a_ss, 1)
                ac.sem_inc(a_x.free, 1)

            def a_main(i, more):
                ac.wait_ge(a_fz, i + 1)
                ac.activation(sq_a[:, 0:S.QR], lat[:, 0:S.QR], ACT.Square, accum_out=st_a[:, 2:3])
                ac.activation(sq_a[:, S.QR:S.QR + S.KR], lat[:, S.QR:S.QR + S.KR], ACT.Square,
                              accum_out=st_a[:, 3:4])
                ac.drain().then_inc(a_lss, 1)
                ac.activation(fz[:, 2, :], fz[:, 1, :], ACT.Exp)
                ac.drain()
                ac.activation(fz[:, 3, :], fz[:, 2, :], ACT.Ln, bias=1.0).then_inc(a_fl, 1)
                ac.wait_ge(a_pp[1].full, a_pp[1].base + 2 * i + 1)
                apart(ac)
                ac.activation(fq_sb[:, :], pp[1][:, :], ACT.Copy, scale=rstd_a[:, bass.ds(i, 1)])\
                    .then_inc(a_pp[1].free, 1)
                ac.wait_ge(a_pp[0].full, a_pp[0].base + 2 * i + 2)
                apart(ac)
                ac.activation(fk_sb[:, :], pp[0][:, :], ACT.Copy, scale=rstd_a[:, bass.ds(i, 1)])\
                    .then_inc(a_pp[0].free, 1)
                if more:
                    a_pre(i + 1)
                hq = H // 2
                for g in range(2):
                    ac.wait_ge(a_pu[g].full, 2 * i + 1)
                    ac.activation(q_sb[:, hq * g:hq * (g + 1), :],
                                  bank_u(g)[:, 0:hq * S.DQ].rearrange("p (h c) -> p h c", h=hq),
                                  ACT.Copy).then_inc(a_pu[g].free, 1)
                for g in range(2):
                    ac.wait_ge(a_pu[g].full, 2 * i + 2)
                    kv = bank_u(g).rearrange("p (h c) -> p h c", h=hq)
                    ac.activation(k_sb[:, hq * g:hq * (g + 1), 0:S.DN], kv[:, :, 0:S.DN], ACT.Copy)
                    ac.activation(
                        v_mla[:, bass.ds(i, 1), hq * g * S.DV:hq * (g + 1) * S.DV].rearrange(
                            "p o (h c) -> p (o h) c", h=hq),
                        kv[:, :, S.DN:], ACT.Copy).then_inc(a_pu[g].free, 1)
                ac.drain().then_inc(a_up, 1)
                ac.wait_ge(a_pp[1].full, a_pp[1].base + 2 * i + 2)
                apart(ac)
                ac.activation(v_fox[:, bass.ds(i, 1), :].rearrange("p o c -> p (o c)"), pp[1][:, :],
                              ACT.Copy, scale=rstd_a[:, bass.ds(i, 1)]).then_inc(a_pp[1].free, 1)
                for g, (b, k, top) in enumerate(A_ST):
                    ac.wait_ge(a_st[g].free, 16 * (i + 1))
                    ac.wait_ge(a_pt[b].full, a_st_use(b, i, k, more))
                    dst = (*st_q, *st_f)[g]
                    ac.activation(dst[:, :, :], pt[b][0:top, :].rearrange("p (h t) -> p h t", h=4),
                                  ACT.Copy).then_inc(a_pt[b].free, 1)
                    ac.drain().then_inc(a_st[g].full, 1)

            a_pre(0)
            with ac.Fori(0, NT - 1) as i:
                a_main(i, True)
            a_main(NT - 1, False)
            barrier(ac, 2)

            for hd in (*b_in, b_cneg, *b_s, *b_p):
                ac.sem_inc(hd.free, 1)

            def b_exp(h, n):
                (y, i), b = B_STEPS[n], n % 2
                L = P * (i + 1)
                ac.wait_ge(b_nm, 2 * NT * h + n + 1)
                ac.wait_ge(b_p[b].free, NT * h + n // 2 + 1)
                src = wide[b] if y == 0 else biased[b]
                e = ac.activation(prob[b][:, 0:L], src[:, 0:L], ACT.Exp, bias=nm[:, n:n + 1], scale=SCALE[y],
                                  accum_out=rs[:, n:n + 1])
                if y == 0:
                    e.then_inc(b_s[b].free, 1)
                ac.drain().then_inc(b_p[b].full, 1)

            def b_second(h, n):
                if len(B_PLAN[n]) > 1:
                    g, b, k = B_PLAN[n][1]
                    ac.wait_ge(b_pt[b].full, b_pt[b].base + B_PT[b] * h + k)
                    m = B_STEPS[n][1] - 3
                    ac.activation(prob_t[n % 2][:, 4:4 + m, :].rearrange("p k t -> p (k t)"), pt[b][:, 0:m * P],
                                  ACT.Copy).then_inc(b_pt[b].free, 1)
                    ac.drain().then_inc(b_pta, 1)

            def b_body(h, last):
                for n in range(2 * NT):
                    if nxt := b_ahead(h, n + 1, last):
                        b_exp(*nxt)
                    b_second(h, n)

            b_exp(0, 0)
            b_loop(ac, b_body)
            barrier(ac, 3)

            ac.sem_inc(c_x.free, 1)
            for g in range(2):
                ac.sem_inc(c_w[g].free, 1)
            for t in range(NT):
                for g in range(2):
                    ac.activation(wide[1][:, g * FW:(g + 1) * FW], o_sb[:, t, g * FW:(g + 1) * FW], ACT.Square,
                                  accum_out=sums[:, CN + 2 * t + g:CN + 2 * t + g + 1])
                ac.drain()
            ac.sem_inc(c_ss, 1)
            for t in range(NT):
                ac.wait_ge(c_h, t + 1)
                ac.activation(wide[1][:, :], h_res[:, t, :], ACT.Square, accum_out=sums[:, XN + t:XN + t + 1])
                ac.drain()
            barrier(ac, 4)

            for hd in (x_s, *x_w):
                ac.sem_inc(hd.free, 1)
            ac.wait_ge(x_rstd, 1)

            def x_square(i):
                ac.wait_ge(x_h, i + 1)
                apart(ac)
                ac.activation(sq_c[:, :], h_res[:, bass.ds(i, 1), :].rearrange("p o c -> p (o c)"), ACT.Square,
                              accum_out=sums[:, bass.ds(RN + i, 1)])
                ac.drain()

            def x_body(i, before):
                for g in range(2):
                    ac.wait_ge(x_pp[g].full, x_pp[g].base + 2 * i + 1)
                    ac.activation(qx_t[:, 4 * g:4 * g + 4, :].rearrange("p k t -> p (k t)"), pp[g][:, :],
                                  ACT.Copy).then_inc(x_pp[g].free, 1)
                ac.drain().then_inc(x_qx, 1)
                ac.wait_ge(x_nm, i + 1)
                apart(ac)
                for hh in range(S.XH):
                    e = ac.activation(px[:, hh, :], wide[0][:, hh * S.M:(hh + 1) * S.M], ACT.Exp,
                                      bias=st_x[:, 8 + hh:9 + hh], scale=xscale[:, bass.ds(i, 1)],
                                      accum_out=st_x[:, 12 + hh:13 + hh])
                e.then_inc(x_s.free, 1)
                ac.drain().then_inc(x_p, 1)
                if before is not None:
                    x_square(before)
                for g in range(2):
                    ac.wait_ge(x_pp[g].full, x_pp[g].base + 2 * i + 2)
                    ac.activation(ox_t[:, 4 * g:4 * g + 4, :].rearrange("p k t -> p (k t)"), pp[g][:, :],
                                  ACT.Copy).then_inc(x_pp[g].free, 1)
                ac.drain().then_inc(x_ox, 1)

            x_body(0, None)
            with ac.Fori(1, NT) as i:
                x_body(i, i - 1)
            x_square(NT - 1)
            barrier(ac, 5)

            ac.wait_ge(r_rstd, 1)

            for t in range(NT):
                ac.activation(rn[t][:, :], h_res[:, t, :], ACT.Copy, scale=rstd[:, RN + t:RN + t + 1])\
                    .then_inc(r_rn, 1)
            ac.wait_ge(r_idx, 1)
            ac.activation(gates[:, :, :], gates[:, :, :], ACT.Exp).then_inc(r_ex, 1)
            barrier(ac, 6)

            for hd in e_dn:
                ac.sem_inc(hd.free, 1)
            ac.wait_ge(ld["bias"], 32)

            def rows_back(i):
                ac.wait_ge(e_left, i + 1)
                for g in range(4):
                    b, k = g % 2, g // 2 + 1
                    ac.wait_ge(e_pt[b].full, turn_out_use(b, i, k))
                    hb, half_d = g // 2, g % 2
                    ac.activation(y_sb[:, hb, half_d * 512:(half_d + 1) * 512], pt[b][:, :],
                                  ACT.Copy).then_inc(e_pt[b].free, 1)
                ac.drain().then_inc(e_y.full, 1)

            def step(i, e, before):
                for m in range(KD):
                    ac.wait_ge(e_glu, KD * i + m + 1)
                    ac.activation(sig[m % 2][:, :], glu[m % 2][:, :], ACT.Sigmoid, scale=1.702).then_inc(e_sig, 1)
                    if m == 1 and before is not None:
                        rows_back(before)
                for m in range(KD):
                    b, k = (m // 2) % 2, m // 4 + 1
                    if m % 2 == 0:
                        ac.wait_ge(e_dn[b].full, 2 * i + k)
                    x = ac.activation(y_t[:, m, :], pp2[b][:, (m % 2) * CAP:(m % 2 + 1) * CAP], ACT.Identity,
                                      bias=b_dn[:, bass.ds(e * KD + m, 1)])
                    if m % 2 == 1:
                        x.then_inc(e_dn[b].free, 1)
                    if m % 4 == 3:
                        ac.sem_inc(e_w[4 + m // 4].free, 1)
                ac.drain().then_inc(e_yt, 1)

            step(0, 0, None)
            with ac.Fori(1, E) as i:
                step(i, i, i - 1)
            rows_back(E - 1)

            def ac_further(i):
                e = ac.value_load(items[0:1, 0, bass.ds(i, 1)], min_val=0, max_val=E - 1)
                step(i, e, None)
                rows_back(i)

            further_blocks(ac, ac_further)
            barrier(ac, 7)

            def f_square(i, b):
                ac.wait_ge(f_acc, i + 1)
                ac.activation(sq_f[:, :], acc[b][:, :], ACT.Square, accum_out=sum_f[:, b:b + 1])
                ac.drain().then_inc(f_ss, 1)

            def f_store(i, b, more):
                if more:
                    f_square(i + 1, 1 - b)
                ac.wait_ge(f_o, i + 1)
                ac.dma_start(out[0, bass.ds(i * P, P), :], of[b][:, :]).then_inc(f_out[b], 16)

            f_square(0, 0)
            pairs(ac, f_store)
            for b in range(2):
                ac.wait_ge(f_out[b], 16 * (NT // 2) + 16)

        @block.tensor
        def _(pe):
            def transposes(dst, srcs, idn):
                for j, s in enumerate(srcs):
                    m = pe.transpose(dst[0:s.shape[-1], j * P:j * P + s.shape[0]], s, idn)
                return m

            def product(dst, parts, n=None):
                n = n or len(parts)
                for k, (l, r_) in enumerate(parts):
                    m = pe.matmul(dst, l, r_, start=(k == 0), stop=(k == n - 1))
                return m

            pe.wait_ge(ld["small"], 64)
            pe.wait_ge(m_n, S.MT)
            n = 0
            for t in range(S.MT):
                for g in range(KD // 4):
                    b = n % 2
                    pe.wait_ge(m_pt[b].free, n // 2 + 1)
                    transposes(pt[b], [mem_n[:, t, (4 * g + j) * P:(4 * g + j + 1) * P] for j in range(4)],
                               ident).then_inc(m_pt[b].full, 1)
                    n += 1
            pe.wait_ge(m_rs, 1 + n)
            pe.wait_ge(ld["w_mem_k"], 16)
            n = 0
            for g in range(KD // 2):
                b = n % 2
                pe.wait_ge(m_pp[b].free, n // 2 + 1)
                for j in range(2):
                    c = 2 * g + j
                    m = product(pp[b][:, j * S.M:(j + 1) * S.M],
                                [(w_mem_k[:, k, c * P:(c + 1) * P], mem_t[:, k, :]) for k in range(KD)])
                m.then_inc(m_pp[b].full, 1)
                n += 1
            pe.wait_ge(ld["w_mem_v"], 16)
            for t in range(S.MT):
                for g in range(D // 512):
                    b = n % 2
                    pe.wait_ge(m_pp[b].free, n // 2 + 1)
                    product(pp[b][:, :], [(mem_t[:, k, t * P:(t + 1) * P], w_mem_v[:, k, g * 512:(g + 1) * 512])
                                          for k in range(KD)]).then_inc(m_pp[b].full, 1)
                    n += 1
            barrier(pe, 1)

            pe.wait_ge(init, 6)
            pe.wait_ge(ld["w_in"], 80)

            def turn(use, b, srcs):
                pe.wait_ge(a_pt[b].free, use)
                return transposes(pt[b], srcs, ident).then_inc(a_pt[b].full, 1)

            def x_in(i):
                pe.wait_ge(a_x.full, 16 * (i + 1))
                for b in range(2):
                    turn(a_in_use(b, i), b, [x_sb[:, j * P:(j + 1) * P] for j in range(4 * b, 4 * b + 4)])

            def project(i, b, k, c0, c1):
                pe.wait_ge(a_pp[b].free, a_pp[b].base + 2 * i + k)
                product(pp[b][:, 0:c1 - c0], [(xt[:, kk, :], w_in[:, kk, c0:c1]) for kk in range(KD)])\
                    .then_inc(a_pp[b].full, 1)

            def a_tile(i, more):
                pe.wait_ge(a_xt, i + 1)
                project(i, 0, 1, 0, S.LAT)
                project(i, 1, 1, S.LAT, S.LAT + FW)
                pe.wait_ge(a_latn, i + 1)
                turn(a_pt[0].base + A_PT[0] * i + 2, 0, [latn[:, j, :] for j in range(3)])
                project(i, 0, 2, S.LAT + FW, S.LAT + 2 * FW)
                pe.wait_ge(a_latt, i + 1)
                hq = H // 2
                for g in range(2):
                    pe.wait_ge(a_pu[g].free, 2 * i + 1)
                    w = hq * S.DQ
                    product(bank_u(g)[:, 0:w], [(lat_t[:, kk, :], w_qu[:, kk, g * w:(g + 1) * w]) for kk in range(2)])\
                        .then_inc(a_pu[g].full, 1)
                for g in range(2):
                    pe.wait_ge(a_pu[g].free, 2 * i + 2)
                    product(bank_u(g), [(lat_t[:, 2, :], w_ku[:, g * 512:(g + 1) * 512])]).then_inc(a_pu[g].full, 1)
                project(i, 1, 2, S.LAT + 2 * FW, S.IN)
                if more:
                    x_in(i + 1)
                pe.wait_ge(a_logf, i + 1)
                pe.wait_ge(a_pc.free, i + 1)
                product(bank_c[0:H, 0:P], [(fz[:, 5, :], tri), (rsum[:, :], ones[:, :])]).then_inc(a_pc.full, 1)
                pe.wait_ge(a_qk, i + 1)
                for g, (b, k, _) in enumerate(A_ST[0:4]):
                    src = (q_sb, k_sb)[g // 2]
                    turn(a_st_use(b, i, k, more), b, [src[:, 4 * (g % 2) + j, :] for j in range(4)])
                for g, (b, k, _) in enumerate(A_ST[4:6]):
                    src = (fq_sb, fk_sb)[g]
                    turn(a_st_use(b, i, k, more), b, [src[:, j * P:(j + 1) * P] for j in range(4)])

            x_in(0)
            with pe.Fori(0, NT - 1) as i:
                a_tile(i, True)
            a_tile(NT - 1, False)
            barrier(pe, 2)

            def scores(h, n, after=None):
                (y, i), b = B_STEPS[n], n % 2
                L = P * (i + 1)
                if n in B_FIRST:
                    pe.wait_ge(b_in[y].full, 32 * (h + 1))
                pe.wait_ge(b_s[b].free, NT * h + n // 2 + 1)
                ql = qt[y][:, i * P:(i + 1) * P]
                for c in range(0, L, 512):
                    w = min(512, L - c)
                    last = c + w == L
                    m = pe.matmul(wide[b][:, c:c + w], ql, kt[y][:, c:c + w], start=True, stop=not last)
                    if c == 0 and after is not None:
                        m.then_inc(after, 1)
                m = pe.matmul(wide[b][:, L - P:L], ident_b[:, :], mask_b[:, :], start=False, stop=True)
                m.then_inc(b_s[b].full, 1)

            second_upto = [sum(len(g) > 1 for g in B_PLAN[:n + 1]) for n in range(2 * NT)]

            def values(h, n):
                (y, i), b = B_STEPS[n], n % 2
                pe.wait_ge(b_ptd, 2 * NT * h + n + 1)
                if len(B_PLAN[n]) > 1:
                    pe.wait_ge(b_pta, B_GRP1 * h + second_upto[n])
                pe.wait_ge(b_po[b].free, b_po[b].base + NT * h + n // 2 + 1)
                v = (v_mla, v_fox)[y]
                for j in range(i + 1):
                    m = pe.matmul(pp[b][:, 0:S.DV], prob_t[b][:, j, :], v[:, j, bass.ds(h * S.DV, S.DV)],
                                  start=j == 0, stop=j == i)
                return m.then_inc(b_po[b].full, 1)

            def b_body(h, last):
                for n in range(2 * NT):
                    (y, i), b = B_STEPS[n], n % 2
                    pe.wait_ge(b_p[b].full, NT * h + n // 2 + 1)
                    for g, tb, k in B_PLAN[n]:
                        pe.wait_ge(b_pt[tb].free, b_pt[tb].base + B_PT[tb] * h + k)
                        blocks = range(4 * g, min(4 * g + 4, i + 1))
                        transposes(pt[tb], [prob[b][:, j * P:(j + 1) * P] for j in blocks], ident)\
                            .then_inc(b_pt[tb].full, 1)
                    if nxt := b_ahead(h, n + 2, last):
                        scores(*nxt, b_p[b].free)
                    if n >= 1:
                        values(h, n - 1)
                values(h, 2 * NT - 1)

            scores(0, 0)
            scores(0, 1)
            b_loop(pe, b_body)
            barrier(pe, 3)

            pe.wait_ge(ld["w_o"], 16)

            def c_turn(i):
                pe.wait_ge(c_row.full, c_row.base + i + 1)
                for g in range(2):
                    pe.wait_ge(c_pt[g].free, c_pt[g].base + i + 1)
                    transposes(pt[g], [row[:, j * P:(j + 1) * P] for j in range(4 * g, 4 * g + 4)], ident)\
                        .then_inc(c_pt[g].full, 1)

            def c_body(i, b, more):
                if more:
                    c_turn(i + 1)
                pe.wait_ge(c_ot, i + 1)
                for g in range(2):
                    for y, dst, hd in ((0, pp[g][:, :], c_pp[g]), (1, pp2[g], c_w[g])):
                        pe.wait_ge(hd.free, hd.base + i + 1)
                        product(dst, [(o_t[b][:, k, :], w_o[:, k, g * 512:(g + 1) * 512])
                                      for k in range(4 * y, 4 * y + 4)]).then_inc(hd.full, 1)

            c_turn(0)
            pairs(pe, c_body)
            barrier(pe, 4)

            pe.wait_ge(ld["w_xq"], 16)
            pe.wait_ge(ld["w_xo"], 16)

            def x_turn(i, kind):
                pe.wait_ge(x_row.full, x_row_use(kind, i))
                for g in range(2):
                    pe.wait_ge(x_pt[g].free, x_pt_use(g, kind, i))
                    transposes(pt[g], [row[:, j * P:(j + 1) * P] for j in range(4 * g, 4 * g + 4)], ident)\
                        .then_inc(x_pt[g].full, 1)

            def x_out(i, done=None):
                pe.wait_ge(x_ox, i + 1)
                for g in range(2):
                    if g == 1 and done is not None:
                        x_turn(done, "R")
                    pe.wait_ge(x_w[g].free, x_w_use(g, "O", i))
                    product(wide[1][:, g * 512:(g + 1) * 512],
                            [(ox_t[:, k, :], w_xo[:, k, g * 512:(g + 1) * 512]) for k in range(KD)])\
                        .then_inc(x_w[g].full, 1)

            def x_logits(i):
                pe.wait_ge(r_rnt, i + 1)
                pe.wait_ge(x_w[0].free, x_w_use(0, "L", i))
                product(wide[1][:, 0:E], [(rn_t[:, k, :], w_r[:, k, :]) for k in range(KD)]).then_inc(x_w[0].full, 1)

            def x_body(i, before, done, more=True):
                pe.wait_ge(x_hnt, i + 1)
                for g in range(2):
                    pe.wait_ge(x_pp[g].free, x_pp[g].base + 2 * i + 1)
                    for j in range(4):
                        c = 4 * g + j
                        m = product(pp[g][:, j * P:(j + 1) * P],
                                    [(w_xq[:, k, c * P:(c + 1) * P], hn_t[:, k, :]) for k in range(KD)])
                    m.then_inc(x_pp[g].full, 1)
                if more:
                    x_turn(i + 1, "T")
                pe.wait_ge(x_qx, i + 1)
                pe.wait_ge(x_s.free, i + 1)
                dc = S.XD // P
                for hh in range(S.XH):
                    m = product(wide[0][:, hh * S.M:(hh + 1) * S.M],
                                [(qx_t[:, hh * dc + c, :], km[:, hh * dc + c, :]) for c in range(dc)])
                m.then_inc(x_s.full, 1)
                if before is not None:
                    x_out(before, done)
                pe.wait_ge(x_pn, i + 1)
                for g in range(2):
                    pe.wait_ge(x_pt[g].free, x_pt_use(g, "P", i))
                    transposes(pt[g], [px[:, c // S.MT, (c % S.MT) * P:(c % S.MT + 1) * P]
                                       for c in range(4 * g, 4 * g + 4)], ident).then_inc(x_pt[g].full, 1)
                if done is not None:
                    x_logits(done)
                pe.wait_ge(x_pxt, i + 1)
                for g in range(2):
                    pe.wait_ge(x_pp[g].free, x_pp[g].base + 2 * i + 2)
                    for j in range(4):
                        c = 4 * g + j
                        m = product(pp[g][:, j * P:(j + 1) * P],
                                    [(vm[:, mt, c * P:(c + 1) * P], px_t[:, (c // dc) * S.MT + mt, :])
                                     for mt in range(S.MT)])
                    m.then_inc(x_pp[g].full, 1)

            pe.wait_ge(ld["w_r"], 16)
            x_turn(0, "T")
            x_body(0, None, None)
            x_body(1, 0, None)
            with pe.Fori(2, NT - 1) as i:
                x_body(i, i - 1, i - 2)
            x_body(NT - 1, NT - 2, NT - 3, False)
            x_out(NT - 1)
            for t in (NT - 2, NT - 1):
                x_turn(t, "R")
                x_logits(t)
            barrier(pe, 5)

            pe.wait_ge(r_sel, 1)
            for t in range(NT):
                m = product(pp[1][:, t * E:(t + 1) * E],
                            [(before_b[:, :], sel_b[:, t, :]), (ones_b[:, :], run_b[:, t, :])])
            m.then_inc(r_rank, 1)
            product(wide[0][:, 0:E], [(ones_b[:, :], run_b[:, NT, :])]).then_inc(r_cnt, 1)

            def e_index(i, e):
                pe.wait_ge(e_hot, i + 1)
                for hb in range(2):
                    m = product(wide[1][:, hb * 4:hb * 4 + 4],
                                [(hot[:, t, hb * P:(hb + 1) * P],
                                  mv4[:, t, bass.ds(e, 1), :].rearrange("p o c -> p (o c)")) for t in range(NT)])
                m.then_inc(e_ix, 1)

            def if_second(n, yes, no):
                if n is None:
                    return yes()
                with pe.If(n > P):
                    yes()
                with pe.Else():
                    no()

            def e_turn_in(i, groups, n=None):
                pe.wait_ge(e_xg, 32 * (i + 1))
                for g in groups:
                    b, k = g % 2, g // 2 + 1
                    pe.wait_ge(e_pt[b].free, turn_in_use(b, i, k))

                    def blocks(halves):
                        for j in range(4):
                            if j % 2 in halves:
                                c = 2 * g + j // 2
                                m = pe.transpose(pt[b][:, j * P:(j + 1) * P], xg[:, j % 2, c * P:(c + 1) * P], ident)
                        m.then_inc(e_pt[b].full, 1)

                    if_second(n, lambda: blocks((0, 1)), lambda: blocks((0,)))

            e_index(0, 0)
            e_turn_in(0, range(4))
            barrier(pe, 6)

            def e_turn_out(i, groups=range(4), n=None):
                pe.wait_ge(e_yt, i + 1)
                for g in groups:
                    b, k = g % 2, g // 2 + 1
                    pe.wait_ge(e_pt[b].free, turn_out_use(b, i, k))
                    hb, hd = g // 2, g % 2
                    srcs = [y_t[:, 4 * hd + j, hb * P:(hb + 1) * P] for j in range(4)]
                    if_second(n if hb else None, lambda: transposes(pt[b], srcs, ident).then_inc(e_pt[b].full, 1),
                              lambda: pe.sem_inc(e_pt[b].full, 1))

            COARSE, FINE = [128, 192, CAP], [*range(112, 209, 8), 224, CAP]

            def by_size(rows_, body, sizes):
                if len(sizes) == 1:
                    body(sizes[0])
                else:
                    mid = len(sizes) // 2
                    with pe.If(rows_ <= sizes[mid - 1]):
                        by_size(rows_, body, sizes[:mid])
                    with pe.Else():
                        by_size(rows_, body, sizes[mid:])

            def e_gate_up(i, m0, m1, w):
                for m in range(m0, m1):
                    c, b = m // 2, m % 2
                    if m % 2 == 0:
                        pe.wait_ge(e_w[c].full, 16 * (i + 1))
                    pe.wait_ge(e_gu[b].free, e_gu[b].base + 4 * i + m // 2 + 1)
                    for u in range(2):
                        x = product(pp[b][:, u * CAP:u * CAP + w],
                                    [(slots[c][:, k, u * CAP + (m % 2) * P:u * CAP + (m % 2 + 1) * P], xe_t[:, k, 0:w])
                                     for k in range(KD)])
                    x.then_inc(e_gu[b].full, 1)

            def e_down(i, m0, m1, w):
                def act(k):
                    pe.wait_ge(e_act, KD * i + k + 1)
                    return act_t[:, k, 0:w]

                for m in range(m0, m1):
                    c, b = 4 + m // 4, (m // 2) % 2
                    if m % 4 == 0:
                        pe.wait_ge(e_w[c].full, 16 * (i + 1))
                    if m % 2 == 0:
                        pe.wait_ge(e_dn[b].free, 2 * i + m // 4 + 1)
                    x = product(pp2[b][:, (m % 2) * CAP:(m % 2) * CAP + w],
                                ((slots[c][:, k, (m % 4) * P:(m % 4 + 1) * P], act_t[:, k, 0:w] if m else act(k))
                                 for k in range(KD)), KD)
                    if m % 2 == 1:
                        x.then_inc(e_dn[b].full, 1)

            def rows_in(i):
                return pe.value_load(items[0:1, 1, bass.ds(i, 1)], min_val=0, max_val=CAP)

            def step(i, before, sizes=COARSE, nxt=None, held=None):
                n = rows_in(i) if held is None else pe.snap(held[0])
                n_before = None if held is None else pe.snap(held[1])
                later = None
                if nxt is None:
                    nxt = pe.value_load(items[0:1, 0, bass.ds(i + 1, 1)], min_val=0, max_val=E - 1)
                pe.wait_ge(e_xt, i + 1)
                by_size(n, lambda w: e_gate_up(i, 0, 2, w), sizes)
                e_index(i + 1, nxt)
                if before is not None:
                    e_turn_out(before, (0, 1))
                by_size(n, lambda w: e_gate_up(i, 2, 3, w), sizes)
                if before is not None:
                    e_turn_out(before, (2, 3), n_before)
                by_size(n, lambda w: e_gate_up(i, 3, 8, w), sizes)
                if held is not None:
                    later = rows_in(i + 1)
                e_turn_in(i + 1, (0, 1), later)
                by_size(n, lambda w: e_down(i, 0, 2, w), sizes)
                e_turn_in(i + 1, (2, 3), later)
                by_size(n, lambda w: e_down(i, 2, 8, w), sizes)
                if held is not None:
                    pe.reg_mov(held[1], n)
                    pe.reg_mov(held[0], later)

            step(0, None)
            held = [pe.alloc_register("rows_held"), pe.alloc_register("rows_before")]
            pe.reg_mov(held[0], rows_in(1))
            pe.reg_mov(held[1], rows_in(0))
            with pe.Fori(1, E - 1) as i:
                step(i, i - 1, FINE, i + 1, held)
            step(E - 1, E - 2)
            e_turn_out(E - 1)

            def pe_further(i):
                step(i, None)
                e_turn_out(i)

            further_blocks(pe, pe_further)
            barrier(pe, 7)

        @block.vector
        def _(ve):
            def scaled(dst, src, g, k, w):
                return ve.tensor_tensor(dst, src.rearrange("p (k t) -> p k t", k=k),
                                        g.unsqueeze(2).to_broadcast([P, k, w]), ALU.mult)

            for hd in (*m_pt, *m_pp):
                ve.sem_inc(hd.free, 1)
            ve.wait_ge(ld["small"], 64)
            n = 0
            for t in range(S.MT):
                for g in range(KD // 4):
                    b = n % 2
                    ve.wait_ge(m_pt[b].full, n // 2 + 1)
                    scaled(mem_t[:, 4 * g:4 * g + 4, t * P:(t + 1) * P], pt[b][:, :], g_mem[:, 4 * g:4 * g + 4], 4, P)\
                        .then_inc(m_pt[b].free, 1)
                    ve.drain().then_inc(m_rs, 1)
                    n += 1
            n = 0
            for g in range(KD // 2):
                b = n % 2
                ve.wait_ge(m_pp[b].full, n // 2 + 1)
                ve.tensor_copy(km[:, 2 * g:2 * g + 2, :].rearrange("p k t -> p (k t)"), pp[b][:, :])\
                    .then_inc(m_pp[b].free, 1)
                n += 1
            for t in range(S.MT):
                for g in range(D // 512):
                    b = n % 2
                    ve.wait_ge(m_pp[b].full, n // 2 + 1)
                    ve.tensor_copy(vm[:, t, g * 512:(g + 1) * 512], pp[b][:, :]).then_inc(m_pp[b].free, 1)
                    n += 1
            barrier(ve, 1)

            ve.wait_ge(ld["rope"], 32)
            ve.memset(rsum[:, :], 0.0)

            def x_copies_a(i):
                for g in range(2):
                    ve.wait_ge(a_pt[g].full, a_in_use(g, i))
                    scaled(xt[:, 4 * g:4 * g + 4, :], pt[g][:, :], g_mix[:, 4 * g:4 * g + 4], 4, P)\
                        .then_inc(a_pt[g].free, 1)
                ve.drain().then_inc(a_xt, 1)
                ve.sem_inc(a_x.free, 1)

            def a_tile(i, more):
                ve.wait_ge(a_rstd, i + 1)
                ve.wait_ge(a_pp[0].full, a_pp[0].base + 2 * i + 1)
                ve.tensor_scalar(lat[:, :], pp[0][:, 0:S.LAT], rstd_a[:, bass.ds(i, 1)], None, ALU.mult)\
                    .then_inc(a_pp[0].free, 1)
                ve.drain()
                ve.tensor_tensor(fz[:, 0, :], lat[:, S.LAT - H:S.LAT], bf_row[:, :], ALU.add)
                ve.drain()
                ve.tensor_scalar(fz[:, 4, :], fz[:, 0, :], -1.0, None, ALU.mult)
                ve.drain()
                ve.tensor_tensor(fz[:, 1, :], fz[:, 0, :], fz[:, 4, :], ALU.min)
                ve.drain().then_inc(a_fz, 1)
                ve.wait_ge(a_lrstd, i + 1)
                ve.tensor_scalar(latn[:, 0:2, :].rearrange("p k c -> p (k c)"), lat[:, 0:S.QR], st_a[:, 6:7], None,
                                 ALU.mult)
                ve.tensor_scalar(latn[:, 2, :], lat[:, S.QR:S.QR + S.KR], st_a[:, 7:8], None, ALU.mult)
                ve.drain().then_inc(a_latn, 1)
                ve.wait_ge(a_fl, i + 1)
                ve.tensor_scalar(fz[:, 4, :], fz[:, 0, :], 0.0, None, ALU.min)
                ve.drain()
                ve.tensor_tensor(fz[:, 5, :], fz[:, 4, :], fz[:, 3, :], ALU.subtract)
                ve.drain().then_inc(a_logf, 1)
                ve.wait_ge(a_pt[0].full, a_pt[0].base + A_PT[0] * i + 2)
                scaled(lat_t[:, :, :], pt[0][:, 0:3 * P], g_lat, 3, P).then_inc(a_pt[0].free, 1)
                ve.drain().then_inc(a_latt, 1)
                ci = cos[:, bass.ds(i, 1), :]
                si = sin[:, bass.ds(i, 1), :]
                hr = S.RO // 2
                kp = lat[:, S.QR + S.KR:S.QR + S.KR + S.RO]
                c1, s1 = ci.rearrange("p o c -> p (o c)"), si.rearrange("p o c -> p (o c)")
                ve.tensor_tensor(krot[:, 0, :], kp, c1, ALU.mult)
                ve.tensor_tensor(krot[:, 1, 0:hr], kp[:, hr:], s1[:, 0:hr], ALU.mult)
                ve.tensor_tensor(krot[:, 1, hr:], kp[:, 0:hr], s1[:, hr:], ALU.mult)
                ve.drain()
                ve.wait_ge(a_up, i + 1)
                ve.tensor_tensor(k_sb[:, :, S.DN:], krot[:, 0:1, :].to_broadcast([P, H, S.RO]),
                                 krot[:, 1:2, :].to_broadcast([P, H, S.RO]), ALU.add)
                qp = q_sb[:, :, S.DN:]
                ve.tensor_tensor(rot[:, 0, :, :], qp, ci.to_broadcast([P, H, S.RO]), ALU.mult)
                ve.tensor_tensor(rot[:, 1, :, 0:hr], qp[:, :, hr:], si[:, :, 0:hr].to_broadcast([P, H, hr]), ALU.mult)
                ve.tensor_tensor(rot[:, 1, :, hr:], qp[:, :, 0:hr], si[:, :, hr:].to_broadcast([P, H, hr]), ALU.mult)
                ve.drain()
                ve.tensor_tensor(qp, rot[:, 0, :, :], rot[:, 1, :, :], ALU.add)
                ve.drain().then_inc(a_qk, 1)
                if more:
                    x_copies_a(i + 1)
                ve.wait_ge(a_pc.full, i + 1)
                ve.wait_ge(a_st[6].free, 16 * (i + 1))
                ve.tensor_scalar(cneg_sb[:, :], bank_c[0:H, 0:P], -1.0 / SCALE[1], None, ALU.mult)\
                    .then_inc(a_st[6].full, 1)
                ve.tensor_tensor(rsum[:, :], rsum[:, :], fz[:, 5, :], ALU.add)
                ve.drain().then_inc(a_pc.free, 1)

            x_copies_a(0)
            with ve.Fori(0, NT - 1) as i:
                a_tile(i, True)
            a_tile(NT - 1, False)
            barrier(ve, 2)

            def row_max(h, n):
                (y, i), b = B_STEPS[n], n % 2
                L = P * (i + 1)
                ve.wait_ge(b_s[b].full, NT * h + n // 2 + 1)
                if y == 0:
                    ve.reduce_max(mx[:, n:n + 1], wide[b][:, 0:L], AX)
                else:
                    if n in B_FIRST:
                        ve.wait_ge(b_cneg.full, 16 * (h + 1))
                    apart(ve)
                    ve.tensor_tensor_reduce(biased[b][:, 0:L], wide[b][:, 0:L], cneg[:, 0:L], 1.0, -3e38, ALU.add,
                                            ALU.max, mx[:, n:n + 1]).then_inc(b_s[b].free, 1)
                ve.drain()
                ve.tensor_scalar(nm[:, n:n + 1], mx[:, n:n + 1], -SCALE[y], None, ALU.mult).then_inc(b_nm, 1)
                if n in B_LAST:
                    ve.sem_inc(b_in[y].free, 1)
                if n == 2 * NT - 1:
                    ve.drain().then_inc(b_cneg.free, 1)

            def attended(h, n):
                (y, i), b = B_STEPS[n], n % 2
                ve.wait_ge(b_po[b].full, b_po[b].base + NT * h + n // 2 + 1)
                ve.tensor_scalar(o_sb[:, i, bass.ds(h * S.DV + y * FW, S.DV)], pp[b][:, 0:S.DV], rr[:, n:n + 1],
                                 None, ALU.mult).then_inc(b_po[b].free, 1)

            def b_body(h, last):
                for n in range(2 * NT):
                    (y, i), b = B_STEPS[n], n % 2
                    g, tb, k = B_PLAN[n][0]
                    m = min(4, i + 1)
                    ve.wait_ge(b_pt[tb].full, b_pt[tb].base + B_PT[tb] * h + k)
                    ve.tensor_copy(prob_t[b][:, 0:m, :].rearrange("p k t -> p (k t)"), pt[tb][:, 0:m * P])\
                        .then_inc(b_pt[tb].free, 1)
                    ve.drain().then_inc(b_ptd, 1)
                    ve.reciprocal(rr[:, n:n + 1], rs[:, n:n + 1])
                    if nxt := b_ahead(h, n + 2, last):
                        row_max(*nxt)
                    ve.drain()
                    if n >= 1:
                        attended(h, n - 1)
                attended(h, 2 * NT - 1)

            row_max(0, 0)
            row_max(0, 1)
            b_loop(ve, b_body)
            barrier(ve, 3)

            def c_copies(i, b):
                for g in range(2):
                    ve.wait_ge(c_pt[g].full, c_pt[g].base + i + 1)
                    scaled(o_t[b][:, 4 * g:4 * g + 4, :], pt[g][:, :], g_out[:, 4 * g:4 * g + 4], 4, P)\
                        .then_inc(c_pt[g].free, 1)
                ve.drain().then_inc(c_ot, 1)
                ve.sem_inc(c_row.free, 1)

            def c_body(i, b, more):
                if more:
                    c_copies(i + 1, 1 - b)
                ve.wait_ge(c_x.full, 16 * (i + 1))
                ht = h_res[:, bass.ds(i, 1), :].rearrange("p o c -> p (o c)")
                for g in range(2):
                    cut = slice(g * 512, (g + 1) * 512)
                    ve.wait_ge(c_pp[g].full, c_pp[g].base + i + 1)
                    ve.scalar_tensor_tensor(out=ht[:, cut], in0=pp[g][:, :], scalar=rstd[:, bass.ds(2 * i + CN, 1)],
                                            in1=x_again[:, cut], op0=ALU.mult, op1=ALU.add).then_inc(c_pp[g].free, 1)
                    ve.drain()
                    ve.wait_ge(c_w[g].full, i + 1)
                    ve.scalar_tensor_tensor(out=ht[:, cut], in0=pp2[g], scalar=rstd[:, bass.ds(2 * i + CN + 1, 1)],
                                            in1=ht[:, cut], op0=ALU.mult, op1=ALU.add).then_inc(c_w[g].free, 1)
                ve.sem_inc(c_x.free, 1)
                ve.drain().then_inc(c_h, 1)

            c_copies(0, 0)
            ve.wait_ge(c_rstd, 1)
            pairs(ve, c_body)
            barrier(ve, 4)

            def x_residual(i):
                ht = h_res[:, bass.ds(i, 1), :].rearrange("p o c -> p (o c)")
                for g in range(2):
                    ve.wait_ge(x_w[g].full, x_w_use(g, "O", i))
                    cut = slice(g * 512, (g + 1) * 512)
                    ve.tensor_tensor(ht[:, cut], ht[:, cut], wide[1][:, cut], ALU.add).then_inc(x_w[g].free, 1)
                ve.drain().then_inc(x_h, 1)

            def x_copies_in(i):
                for g in range(2):
                    ve.wait_ge(x_pt[g].full, x_pt_use(g, "T", i))
                    scaled(hn_t[:, 4 * g:4 * g + 4, :], pt[g][:, :], g_cross[:, 4 * g:4 * g + 4], 4, P)\
                        .then_inc(x_pt[g].free, 1)
                ve.drain().then_inc(x_hnt, 1)
                ve.sem_inc(x_row.free, 1)

            def r_copies(i):
                for g in range(2):
                    ve.wait_ge(x_pt[g].full, x_pt_use(g, "R", i))
                    scaled(rn_t[:, 4 * g:4 * g + 4, :], pt[g][:, :], g_ffn[:, 4 * g:4 * g + 4], 4, P)\
                        .then_inc(x_pt[g].free, 1)
                ve.drain().then_inc(r_rnt, 1)
                ve.sem_inc(x_row.free, 1)

            def r_logits(i):
                ve.wait_ge(x_w[0].full, x_w_use(0, "L", i))
                ve.tensor_copy(lg[:, bass.ds(i, 1), :].rearrange("p o e -> p (o e)"), wide[1][:, 0:E])\
                    .then_inc(x_w[0].free, 1)

            def x_body(i, before, done, more=True):
                if more:
                    x_copies_in(i + 1)
                ve.wait_ge(x_s.full, i + 1)
                ve.tensor_reduce(st_x[:, 4:4 + S.XH], wide[0][:, :].rearrange("p (h m) -> p h m", h=S.XH), AX, ALU.max)
                ve.drain()
                ve.tensor_scalar(st_x[:, 8:8 + S.XH], st_x[:, 4:4 + S.XH], xscale[:, bass.ds(i, 1)], -1.0,
                                 ALU.mult, ALU.mult)\
                    .then_inc(x_nm, 1)
                ve.wait_ge(x_p, i + 1)
                ve.reciprocal(st_x[:, 16:16 + S.XH], st_x[:, 12:12 + S.XH])
                ve.drain()
                ve.tensor_tensor(px[:, :, :], px[:, :, :],
                                 st_x[:, 16:16 + S.XH].unsqueeze(2).to_broadcast([P, S.XH, S.M]), ALU.mult)\
                    .then_inc(x_pn, 1)
                if done is not None:
                    r_copies(done)
                if before is not None:
                    x_residual(before)
                for g in range(2):
                    ve.wait_ge(x_pt[g].full, x_pt_use(g, "P", i))
                    ve.tensor_copy(px_t[:, 4 * g:4 * g + 4, :].rearrange("p k t -> p (k t)"), pt[g][:, :])\
                        .then_inc(x_pt[g].free, 1)
                ve.drain().then_inc(x_pxt, 1)
                if done is not None:
                    r_logits(done)

            ve.wait_ge(x_rstd, 1)
            x_copies_in(0)
            x_body(0, None, None)
            x_body(1, 0, None)
            with ve.Fori(2, NT - 1) as i:
                x_body(i, i - 1, i - 2)
            x_body(NT - 1, NT - 2, NT - 3, False)
            x_residual(NT - 1)
            for t in (NT - 2, NT - 1):
                r_copies(t)
                r_logits(t)
            barrier(ve, 5)

            ve.memset(run_b[:, 0, :], 0.0)
            for j in range(S.TOP):
                ve.memset(jrow[:, j:j + 1], float(j))
            ve.wait_ge(r_rstd, 1)

            ve.tensor_tensor(lg[:, :, :], lg[:, :, :], rstd[:, RN:RN + NT].unsqueeze(2).to_broadcast([P, NT, E]),
                             ALU.mult)
            ve.drain()
            ve.tensor_tensor(lg[:, :, :], lg[:, :, :], br_row[:, :].unsqueeze(1).to_broadcast([P, NT, E]), ALU.add)
            ve.drain()
            for t in range(NT):
                ve.max(val8[:, t, :], lg[:, t, :])
            ve.drain()
            for t in range(NT):
                ve.max_index(idx8[:, t, :], val8[:, t, :], lg[:, t, :])
            ve.drain()
            top = val8[:, :, 0:S.TOP]
            ve.tensor_tensor(gates[:, :, :], top, val8[:, :, 0:1].to_broadcast([P, NT, S.TOP]), ALU.subtract)
            ve.tensor_copy(idxf[:, :, :], idx8[:, :, :])
            ve.drain().then_inc(r_idx, 1)
            ve.tensor_tensor(eq[:, :, :, :], iota[:, 0:E].unsqueeze(1).unsqueeze(1).to_broadcast([P, NT, S.TOP, E]),
                             idxf[:, :, 0:S.TOP].unsqueeze(3).to_broadcast([P, NT, S.TOP, E]), ALU.is_equal)
            ve.drain()
            ve.tensor_reduce(sel[:, :, :], eq[:, :, :, :].rearrange("p t j e -> p t e j"), AX, ALU.add)
            ve.drain()
            ve.tensor_copy(sel_b[:, :, :], sel[:, :, :])
            for t in range(NT):
                ve.tensor_tensor(run_b[:, t + 1, :], run_b[:, t, :], sel[:, t, :], ALU.add)
                ve.drain()
            ve.sem_inc(r_sel, 1)
            ve.tensor_tensor(eqj[:, :, :, :], eq[:, :, :, :],
                             jrow[:, :].unsqueeze(1).unsqueeze(3).to_broadcast([P, NT, S.TOP, E]), ALU.mult)
            ve.drain()
            with nc.allow_low_precision(reason="choices 0 to 3 are exact in bfloat16"):
                ve.tensor_reduce(mv4[:, :, :, 2:3].rearrange("p t e c -> p t (e c)"),
                                 eqj[:, :, :, :].rearrange("p t j e -> p t e j"), AX, ALU.add)
            keys = key[:, :, :].rearrange("p t e -> p (t e)")
            ve.wait_ge(r_rank, 1)
            ve.scalar_tensor_tensor(out=keys, in0=pp[1][:, 0:NT * E], scalar=1.0,
                                    in1=sel[:, :, :].rearrange("p t e -> p (t e)"), op0=ALU.add, op1=ALU.mult)
            ve.wait_ge(r_cnt, 1)
            ve.tensor_copy(cnt[:, :], wide[0][:, 0:E])
            ve.drain()
            ve.tensor_scalar(keys, keys, -1.0, None, ALU.add)
            def one_hot(i, e, t):
                return ve.tensor_scalar(hot[:, t, :], iota, shift[:, bass.ds(i, 1)],
                                        key[:, t, bass.ds(e, 1)], ALU.add, ALU.is_equal)

            def indices(i):
                ve.wait_ge(e_ix, i + 1)
                ve.tensor_copy(ix[:, :, :], wide[1][:, 0:8].rearrange("p (h c) -> p h c", h=2))
                ve.drain()
                ve.tensor_tensor(ixt[:, :], ix[:, :, 0], ix[:, :, 1], ALU.add)
                ve.tensor_scalar(ixo[:, :], ix[:, :, 3], -float(8 * T), float(8 * T), ALU.mult, ALU.add)
                ve.drain()
                ve.tensor_tensor(gidx[:, :], ixt[:, :], ixo[:, :], ALU.add)
                ve.scalar_tensor_tensor(out=ixs[:, :], in0=ixt[:, :], scalar=float(S.TOP), in1=ix[:, :, 2],
                                        op0=ALU.mult, op1=ALU.add)
                ve.drain()
                ve.tensor_tensor(ixs[:, :], ixs[:, :], ixo[:, :], ALU.add)
                ve.drain()

            def x_copies(i):
                for g in range(4):
                    b, k = g % 2, g // 2 + 1
                    ve.wait_ge(e_pt[b].full, turn_in_use(b, i, k))
                    scaled(xe_t[:, 2 * g:2 * g + 2, :], pt[b][:, :], g_ffn[:, 2 * g:2 * g + 2], 2, CAP)\
                        .then_inc(e_pt[b].free, 1)
                ve.drain().then_inc(e_xt, 1)

            def hots(i, e):
                for t in range(NT):
                    one_hot(i, e, t)
                ve.drain().then_inc(e_hot, 1)

            ve.memset(shift[:, 0:E], 0.0)
            ve.drain()
            hots(0, 0)
            ve.tensor_copy(items[:, 0, 0:E], iota[:, 0:E])
            ve.tensor_scalar(items[:, 1, 0:E], cnt[:, :], float(CAP), None, ALU.min)
            indices(0)
            ve.sem_inc(e_idx, 1)
            ve.tensor_copy(ixp[:, :], ixs[:, :])
            ve.memset(items[:, 2, 0:E], 1)
            for b in range(3):
                ve.tensor_scalar(more[:, b, :], cnt[:, :], float(CAP * (b + 1)), None, ALU.is_gt)
            ve.drain()
            ve.tensor_tensor(more[:, 0, :], more[:, 0, :], more[:, 1, :], ALU.add)
            ve.drain()
            ve.tensor_tensor(more[:, 0, :], more[:, 0, :], more[:, 2, :], ALU.add)
            ve.memset(more[:, 1, :], 1.0)
            ve.drain()
            ve.tensor_tensor_scan(more[:, 2, :], more[:, 1, :], more[:, 0, :], 0.0, ALU.mult, ALU.add)
            ve.drain()
            q_row = iota[:, 0:NQ]
            total = more[:, 2, :].unsqueeze(1).to_broadcast([P, NQ, E])
            ve.tensor_tensor(le[:, :, :], total, q_row.unsqueeze(2).to_broadcast([P, NQ, E]), ALU.is_le)
            ve.drain()
            ve.tensor_tensor(le2[:, :, :], le[:, :, :], more[:, 0:1, :].to_broadcast([P, NQ, E]), ALU.mult)
            ve.tensor_reduce(ov[:, 0, :], le[:, :, :], AX, ALU.add)
            ve.drain()
            ve.tensor_reduce(ov[:, 1, :], le2[:, :, :], AX, ALU.add)
            ve.tensor_scalar(ov[:, 2, :], ov[:, 0, :], float(E), None, ALU.is_lt)
            ve.drain()
            ve.tensor_tensor(ov[:, 3, :], q_row, ov[:, 1, :], ALU.subtract)
            ve.tensor_tensor(le[:, :, :], iota[:, 0:E].unsqueeze(1).to_broadcast([P, NQ, E]),
                             ov[:, 0, :].unsqueeze(2).to_broadcast([P, NQ, E]), ALU.is_equal)
            ve.drain()
            ve.tensor_scalar(ov[:, 3, :], ov[:, 3, :], 1.0, float(CAP), ALU.add, ALU.mult)
            ve.tensor_tensor(le2[:, :, :], le[:, :, :], cnt[:, :].unsqueeze(1).to_broadcast([P, NQ, E]), ALU.mult)
            ve.drain()
            ve.tensor_reduce(ov[:, 4, :], le2[:, :, :], AX, ALU.add)
            ve.drain()
            ve.tensor_tensor(ov[:, 4, :], ov[:, 4, :], ov[:, 3, :], ALU.subtract)
            ve.tensor_scalar(shift[:, E:E + NQ], ov[:, 3, :], 0.0, None, ALU.add)
            ve.tensor_scalar(ov[:, 5, :], ov[:, 0, :], float(E - 1), None, ALU.min)
            ve.drain()
            ve.tensor_scalar(ov[:, 4, :], ov[:, 4, :], 0.0, float(CAP), ALU.max, ALU.min)
            ve.tensor_copy(items[:, 0, E:E + NQ], ov[:, 5, :])
            ve.tensor_copy(items[:, 2, E:E + NQ], ov[:, 2, :])
            ve.tensor_scalar(ov[:, 6, :], ov[:, 2, :], -float(8 * T), float(8 * T), ALU.mult, ALU.add)
            ve.drain()
            ve.tensor_copy(items[:, 1, E:E + NQ], ov[:, 4, :])
            ve.tensor_tensor(shift[:, E:E + NQ], shift[:, E:E + NQ], ov[:, 6, :], ALU.add)
            ve.wait_ge(r_ex, 1)
            ve.tensor_reduce(gate_sum[:, :], gates[:, :, :], AX, ALU.add)
            ve.drain()
            ve.reciprocal(gate_sum[:, :], gate_sum[:, :])
            ve.drain()
            ve.tensor_tensor(gates[:, :, :], gates[:, :, :], gate_sum[:, :].unsqueeze(2).to_broadcast([P, NT, S.TOP]),
                             ALU.mult)
            x_copies(0)
            barrier(ve, 6)
            hots(1, 1)

            def step(i, e):
                nxt = ve.value_load(items[0:1, 0, bass.ds(i + 2, 1)], min_val=0, max_val=E - 1)
                for m in range(KD):
                    b = m % 2
                    ve.wait_ge(e_gu[b].full, e_gu[b].base + 4 * i + m // 2 + 1)
                    ve.tensor_scalar(glu[b][:, :], pp[b][:, 0:CAP], b_gu[:, bass.ds(e * 2 * KD + 2 * m, 1)], 7.0,
                                     ALU.add, ALU.min).then_inc(e_glu, 1)
                    ve.tensor_scalar(lin[b][:, :], pp[b][:, CAP:2 * CAP], b_gu[:, bass.ds(e * 2 * KD + 2 * m + 1, 1)],
                                     7.0, ALU.add, ALU.min).then_inc(e_gu[b].free, 1)
                    if m % 2 == 1:
                        ve.sem_inc(e_w[m // 2].free, 1)
                    ve.drain()
                    ve.tensor_scalar(lin[b][:, :], lin[b][:, :], -7.0, 1.0, ALU.max, ALU.add)
                    ve.drain()
                    ve.tensor_tensor(lin[b][:, :], lin[b][:, :], glu[b][:, :], ALU.mult)
                    ve.drain()
                    ve.wait_ge(e_sig, KD * i + m + 1)
                    ve.tensor_tensor(act_t[:, m, :], lin[b][:, :], sig[b][:, :], ALU.mult).then_inc(e_act, 1)
                    if m == 1:
                        indices(i + 1)
                        ve.sem_inc(e_idx, 1)
                    if m == 6:
                        ve.wait_ge(e_left, i + 1)
                        ve.tensor_copy(sidx[:, :], ixp[:, :])
                        ve.drain()
                        ve.tensor_copy(ixp[:, :], ixs[:, :])
                ve.drain()
                x_copies(i + 1)
                hots(i + 2, nxt)

            ve.wait_ge(ld["bias"], 32)
            with ve.Fori(0, E) as i:
                step(i, i)

            def ve_further(i):
                e = ve.value_load(items[0:1, 0, bass.ds(i, 1)], min_val=0, max_val=E - 1)
                step(i, e)

            further_blocks(ve, ve_further)
            for b in range(2):
                ve.sem_inc(f_y[b].free, 2)
            barrier(ve, 7)

            ve.wait_ge(ld["g_fin"], 16)

            def f_sum(i, b):
                ve.wait_ge(f_y[b].full, 8 * (i - b) + 16)
                ht = h_res[:, bass.ds(i, 1), :].rearrange("p o c -> p (o c)")
                for j in range(S.TOP):
                    g = gates[:, bass.ds(i, 1), j:j + 1].rearrange("p o c -> p (o c)")
                    ve.scalar_tensor_tensor(out=acc[b][:, :], in0=ye[b][:, j, :], scalar=g,
                                            in1=ht if j == 0 else acc[b][:, :], op0=ALU.mult, op1=ALU.add)
                    if j < S.TOP - 1:
                        ve.drain()
                ve.drain().then_inc(f_acc, 1)
                ve.sem_inc(f_y[b].free, 2)

            def f_body(i, b, more):
                if more:
                    f_sum(i + 1, 1 - b)
                ve.wait_ge(f_rstd, i + 1)
                ve.wait_ge(f_out[b], 8 * (i - b) + 16)
                ve.scalar_tensor_tensor(out=of[b][:, :], in0=acc[b][:, :], scalar=rstd_f[:, b:b + 1], in1=g_fin[:, :],
                                        op0=ALU.mult, op1=ALU.mult)
                ve.drain().then_inc(f_o, 1)

            f_sum(0, 0)
            pairs(ve, f_body)


def kernel(**inputs):
    import numpy as _np
    import concourse.bacc as _bacc
    from concourse import mybir as _mybir
    from concourse.bass_utils import run_bass_kernel_spmd as _run

    v = {n: _np.asarray(w) for n, w in inputs.items()}
    S = shapes(v["x"], v["mem"], v["w_q_up"], v["w_router"], v["w_in"])
    C = _np.ascontiguousarray

    def chunks(g):
        return g.reshape(-1, P).T

    at = _np.arange(P)
    const = [_np.eye(P), at[:, None] <= at[None, :], _np.where(at[:, None] < at[None, :], MASKED, 0.0),
             _np.tile(_np.arange(S.CAP), (P, 1)), at[:, None]]
    const = C(_np.concatenate([c.astype(_np.float32) for c in const], axis=1))
    S.NCONST = const.shape[1]
    half = S.RO // 2
    inv = _np.float32(10000.0) ** (-_np.arange(half, dtype=_np.float32) / _np.float32(half))
    angle = _np.arange(S.T, dtype=_np.float32)[:, None] * inv[None, :].astype(_np.float32)
    cos, sin = _np.cos(angle).astype(_np.float32), _np.sin(angle).astype(_np.float32)

    E, KD, D = S.E, S.KD, S.D
    wgu = v["w_gate_up"][0].reshape(E, KD, P, 4, 256, 2).transpose(0, 3, 2, 1, 5, 4).reshape(E * 4, P, KD, 512)
    wdn = v["w_down"][0].reshape(E, KD, P, 2, 512).transpose(0, 3, 2, 1, 4).reshape(E * 2, P, KD, 512)
    bgu = v["b_gate_up"][0].reshape(E, KD, P, 2).transpose(2, 0, 1, 3).reshape(P, E * 2 * KD)
    bdn = v["b_down"][0].reshape(E, KD, P).transpose(2, 0, 1).reshape(P, E * KD)
    gains = _np.concatenate([chunks(v["ln_mix"][0]), chunks(v["ln_cross"][0]), chunks(v["mem_norm"][0]),
                             chunks(v["ln_ffn"][0]), chunks(v["q_norm"][0]), chunks(v["kv_norm"][0]),
                             chunks(v["g_out_mla"][0]), chunks(v["g_out_fox"][0])], axis=1)
    feed = {
        "const": const, "cos": C(_np.concatenate([cos, cos], 1)), "sin": C(_np.concatenate([-sin, sin], 1)),
        "gains": C(gains), "w_gu": C(wgu), "w_dn": C(wdn), "b_gu": C(bgu), "b_dn": C(bdn),
    }
    for n in ("x", "mem", "w_in", "w_q_up", "w_kv_up", "b_forget", "w_o", "w_xq", "w_mem_kv", "w_xo", "w_router",
              "b_router", "ln_final"):
        feed[n] = C(v[n])

    nc = _bacc.Bacc("TRN2", target_bir_lowering=False, num_devices=1)
    arrays = {f"in_{n}": w for n, w in feed.items()}
    a = {n: nc.dram_tensor(f"in_{n}", w.shape, _mybir.dt.from_np(w.dtype), kind="ExternalInput").ap()
         for n, w in feed.items()}
    out = nc.dram_tensor("out_h", v["x"].shape, F32, kind="ExternalOutput").ap()
    build(nc, S, a, out)
    r = _run(nc, [arrays], core_ids=[0])
    return r.results[0]["out_h"]
```
